# Optimizing a Trainium2 kernel written in Bass

```python
import math
import jax, jax.numpy as jnp
from jax import lax
import numpy as np

D_MODEL = 2048
BATCH = 1
SEQ = 256
DEPTH = 1

CHUNK = 64
EPS = 1e-6
ATTN_WIDTH = D_MODEL // 2
HEAD_DIM = 64
N_Q_HEADS = ATTN_WIDTH // HEAD_DIM
N_KV_HEADS = max(1, N_Q_HEADS // 8)
Q_PER_KV = N_Q_HEADS // N_KV_HEADS
WINDOW = 128
WINDOW_CHUNKS = max(1, WINDOW // CHUNK)
KEY_BLOCK = WINDOW_CHUNKS * CHUNK
RET_WIDTH = D_MODEL - ATTN_WIDTH
RET_HEAD_DIM = 256
N_RET_HEADS = RET_WIDTH // RET_HEAD_DIM
D_FF = 4 * D_MODEL
KV_WIDTH = N_KV_HEADS * HEAD_DIM
IN_COLS = ATTN_WIDTH + 2 * KV_WIDTH + 4 * RET_WIDTH
N_MOD = 6

kernel_name = "hybrid_swa_sink_retention_block"

def _alibi_slopes(n_heads):
    return np.array([2.0 ** (-8.0 * (h + 1) / n_heads) for h in range(n_heads)], dtype=np.float32)

def _retention_log_gammas(n_heads):
    return np.log(1.0 - 2.0 ** (-5.0 - np.arange(n_heads, dtype=np.float64))).astype(np.float32)

def rmsnorm(x, g):
    xf = x.astype(jnp.float32)
    y = xf * lax.rsqrt(jnp.mean(xf * xf, axis=-1, keepdims=True) + EPS)
    return (y * g.astype(jnp.float32)).astype(x.dtype)

def modulate(h, shift, scale):
    return h * (1.0 + scale[:, None, :]) + shift[:, None, :]

def _band(t, n_chunks):
    parts = []
    for w in range(WINDOW_CHUNKS - 1, -1, -1):
        shifted = jnp.pad(t, ((0, 0), (w, 0), (0, 0), (0, 0), (0, 0)))[:, :n_chunks]
        parts.append(shifted)
    return jnp.concatenate(parts, axis=2)

def sliding_window_attention(q, k, v, sinks):
    b, t = q.shape[0], q.shape[1]
    n_chunks = t // CHUNK
    qc = q.reshape(b, n_chunks, CHUNK, N_KV_HEADS, Q_PER_KV, HEAD_DIM)
    kb = _band(k.reshape(b, n_chunks, CHUNK, N_KV_HEADS, HEAD_DIM), n_chunks)
    vb = _band(v.reshape(b, n_chunks, CHUNK, N_KV_HEADS, HEAD_DIM), n_chunks)
    scores = jnp.einsum('bcqhgd,bckhd->bchgqk', qc, kb).astype(jnp.float32) * (HEAD_DIM ** -0.5)
    q_pos = (WINDOW_CHUNKS - 1) * CHUNK + np.arange(CHUNK)
    k_pos = np.arange(KEY_BLOCK)
    dist = jnp.asarray(np.abs(q_pos[:, None] - k_pos[None, :]).astype(np.float32))
    slopes = jnp.asarray(_alibi_slopes(N_Q_HEADS)).reshape(N_KV_HEADS, Q_PER_KV)
    scores = scores - slopes[:, :, None, None] * dist
    key_chunk = jnp.arange(n_chunks)[:, None] - (WINDOW_CHUNKS - 1) + jnp.asarray(k_pos // CHUNK)[None, :]
    valid = (key_chunk >= 0)[None, :, None, None, None, :]
    scores = jnp.where(valid, scores, jnp.float32(-1e30))
    s = sinks.astype(jnp.float32).reshape(N_KV_HEADS, Q_PER_KV)[None, None, :, :, None, None]
    m = jnp.maximum(jnp.max(scores, axis=-1, keepdims=True), s)
    p = jnp.exp(scores - m)
    probs = p / (jnp.sum(p, axis=-1, keepdims=True) + jnp.exp(s - m))
    out = jnp.einsum('bchgqk,bckhd->bcqhgd', probs.astype(v.dtype), vb)
    return out.reshape(b, t, N_Q_HEADS * HEAD_DIM)

def retention(q, k, v):
    b, t = q.shape[0], q.shape[1]
    n_chunks = t // CHUNK
    f32 = jnp.float32

    def to_chunks(a):
        return a.astype(f32).reshape(b, n_chunks, CHUNK, N_RET_HEADS, RET_HEAD_DIM).transpose(1, 0, 3, 2, 4)

    qc, kc, vc = to_chunks(q), to_chunks(k) * (RET_HEAD_DIM ** -0.5), to_chunks(v)
    log_g = jnp.asarray(_retention_log_gammas(N_RET_HEADS))
    idx = jnp.arange(CHUNK, dtype=f32)
    intra_decay = jnp.exp(log_g[:, None, None] * jnp.abs(idx[:, None] - idx[None, :]))
    cross_decay = jnp.exp(log_g[:, None] * (idx + 1.0))
    state_decay = jnp.exp(log_g[:, None] * (CHUNK - 1.0 - idx))
    chunk_decay = jnp.exp(log_g * CHUNK)

    def step(state, xs):
        qi, ki, vi = xs
        a = jnp.einsum('bhqd,bhkd->bhqk', qi, ki) * intra_decay[None]
        o = jnp.einsum('bhqk,bhkv->bhqv', a, vi)
        o = o + jnp.einsum('bhqd,bhdv->bhqv', qi, state) * cross_decay[None, :, :, None]
        state = state * chunk_decay[None, :, None, None] + jnp.einsum(
            'bhkd,bhkv->bhdv', ki * state_decay[None, :, :, None], vi)
        return state, o

    s0 = jnp.zeros((b, N_RET_HEADS, RET_HEAD_DIM, RET_HEAD_DIM), f32)
    _, outs = lax.scan(step, s0, (qc, kc, vc))
    return outs.transpose(1, 0, 3, 2, 4).reshape(b, t, N_RET_HEADS, RET_HEAD_DIM)

def head_group_norm(y, g):
    mu = jnp.mean(y, axis=-1, keepdims=True)
    var = jnp.mean(jnp.square(y - mu), axis=-1, keepdims=True)
    yn = (y - mu) * lax.rsqrt(var + EPS)
    return yn.reshape(y.shape[0], y.shape[1], -1) * g.astype(jnp.float32)

def setup_inputs(seed: int = 0) -> dict:
    key = jax.random.key(seed)
    ks = jax.random.split(key, 16)
    f32 = jnp.float32
    nrm = lambda k, shape, s: jax.random.normal(k, shape, f32) * s
    return {
        "x": nrm(ks[0], (BATCH, SEQ, D_MODEL), 1.0),
        "c": nrm(ks[1], (BATCH, D_MODEL), 1.0),
        "w_ada": nrm(ks[2], (DEPTH, D_MODEL, N_MOD * D_MODEL), 0.5 * D_MODEL ** -0.5),
        "b_ada": nrm(ks[3], (DEPTH, N_MOD * D_MODEL), 0.01),
        "g_mix": 1.0 + nrm(ks[4], (DEPTH, D_MODEL), 0.02),
        "w_in": nrm(ks[5], (DEPTH, D_MODEL, IN_COLS), D_MODEL ** -0.5),
        "beta_attn": 1.0 + nrm(ks[6], (DEPTH, ATTN_WIDTH), 0.02),
        "sinks": nrm(ks[7], (DEPTH, N_Q_HEADS), 1.0),
        "g_ret": 1.0 + nrm(ks[8], (DEPTH, RET_WIDTH), 0.02),
        "w_out": nrm(ks[9], (DEPTH, D_MODEL, D_MODEL), D_MODEL ** -0.5),
        "g_ffn": 1.0 + nrm(ks[10], (DEPTH, D_MODEL), 0.02),
        "w1": nrm(ks[11], (DEPTH, D_MODEL, D_FF), D_MODEL ** -0.5),
        "w2": nrm(ks[12], (DEPTH, D_FF, D_MODEL), D_FF ** -0.5),
        "g_final": 1.0 + nrm(ks[13], (D_MODEL,), 0.02),
    }

def reference(x, c, w_ada, b_ada, g_mix, w_in, beta_attn, sinks, g_ret, w_out, g_ffn, w1, w2, g_final):
    b, t, _ = x.shape
    for layer in range(DEPTH):
        mod = c @ w_ada[layer] + b_ada[layer]
        sh1, sc1, gt1, sh2, sc2, gt2 = jnp.split(mod, N_MOD, axis=-1)

        h = modulate(rmsnorm(x, g_mix[layer]), sh1, sc1)
        proj = h @ w_in[layer]
        cuts = np.cumsum([ATTN_WIDTH, KV_WIDTH, KV_WIDTH, RET_WIDTH, RET_WIDTH, RET_WIDTH])
        qa, ka, va, qr, kr, vr, gr = jnp.split(proj, cuts, axis=-1)
        ya = sliding_window_attention(
            qa.reshape(b, t, N_Q_HEADS, HEAD_DIM),
            ka.reshape(b, t, N_KV_HEADS, HEAD_DIM),
            va.reshape(b, t, N_KV_HEADS, HEAD_DIM),
            sinks[layer]) * beta_attn[layer]
        yr = retention(qr.reshape(b, t, N_RET_HEADS, RET_HEAD_DIM),
                       kr.reshape(b, t, N_RET_HEADS, RET_HEAD_DIM),
                       vr.reshape(b, t, N_RET_HEADS, RET_HEAD_DIM))
        yr = (jax.nn.silu(gr.astype(jnp.float32)) * head_group_norm(yr, g_ret[layer])).astype(x.dtype)
        y = jnp.concatenate([ya.astype(x.dtype), yr], axis=-1) @ w_out[layer]
        x = x + gt1[:, None, :] * y

        h2 = modulate(rmsnorm(x, g_ffn[layer]), sh2, sc2)
        f = jnp.square(jax.nn.relu(h2 @ w1[layer])) @ w2[layer]
        x = x + gt2[:, None, :] * f
    return rmsnorm(x, g_final)


_drawn_inputs = setup_inputs


def setup_inputs(seed=0):
    import zlib

    import numpy as np

    out = dict(_drawn_inputs(seed))
    spreads = {}
    factors = {'b_ada': 2.878,
     'g_mix': 5.408,
     'beta_attn': 25.723,
     'sinks': 8.0,
     'g_ret': 38.336,
     'g_ffn': 18.901,
     'g_final': 7.88}
    for name, (base, spread) in spreads.items():
        noise = np.random.default_rng([zlib.crc32(name.encode()), seed]).standard_normal(out[name].shape)
        drawn = base * np.exp(spread * noise) if base else spread * noise
        out[name] = __import__('jax').numpy.asarray(drawn.astype(out[name].dtype))
    for name, factor in factors.items():
        out[name] = (out[name] * factor).astype(out[name].dtype)
    return out
```

```python
from contextlib import ExitStack

import numpy as np

import concourse.bass as bass
from concourse import mybir

F32 = mybir.dt.float32
F32R = mybir.dt.float32r
ACT = mybir.ActivationFunctionType
ALU = mybir.AluOpType
AX_X = mybir.AxisListType.X

P = 128
D = 2048
T = 256
TT = T // P
KT = D // P
CHUNK = 64
HEAD = 64
KV_COLS = 128
ATTN = D // 2
RET_HEAD = 256
RET_HEADS = (D - ATTN) // RET_HEAD
PAIRS = ATTN // P
FF = 4 * D
EPS = 1e-6
IN_COLS = ATTN + 2 * KV_COLS + 4 * (D - ATTN)
G = 2048
STAGES = 4
FEAT_COLS = 256
TOK_COLS = 512
STRIPS = D // TOK_COLS

Q0 = 0
KV0 = ATTN
QR0 = ATTN + 2 * KV_COLS
KR0 = QR0 + D - ATTN
VR0 = KR0 + D - ATTN
GR0 = VR0 + D - ATTN

JOBS = [("feat", KV0)]
JOBS += [("feat", Q0 + FEAT_COLS * n) for n in range(4)]
JOBS += [("feat", QR0 + FEAT_COLS * n) for n in range(8)]
JOBS += [("tok", VR0 + TOK_COLS * n) for n in range(2)]
JOBS += [("tok", GR0 + TOK_COLS * n) for n in range(2)]
JOBS += [("out_attn", TOK_COLS * n) for n in range(STRIPS)]
JOBS += [("out_ret", TOK_COLS * n) for n in range(STRIPS)]
J_Q, J_QKR, J_VR, J_GR, J_OA, J_OR, J_MLP = 1, 5, 13, 15, 17, 21, 25
N_GROUPS = [4 if kind == "tok" else 2 for kind, _ in JOBS]
FIRST = [sum(N_GROUPS[:j]) for j in range(len(JOBS) + 1)]
SUPER = FF // D
G_MLP = FIRST[J_MLP]
F_JOBS = D // FEAT_COLS
B_GROUPS = 2 * F_JOBS
T_GROUPS = 4

SH1, SC1, GT1, SH2, SC2, GT2 = (n * D for n in range(6))
FIRST_UNITS = [(SC1, 0), (SH1, 1)]
POOL_UNITS = [(GT1, 0), (SH2, 1), (SC2, 1), (GT2, 0)]
PRE = 2 * KT

V_MIX, V_FFN, V_BETA, V_GRET, V_C = 0, 16, 32, 40, 48


def key_count(t):
    return P * (t + 1)


def build(nc, x, c, w_ada, b_ada, g_mix, w_in, beta_attn, sinks, g_ret, w_out, g_ffn, w1, w2,
          g_final, consts, decay_in, out):
    with ExitStack() as ctx:
        base = 16512
        place = {"at": base}

        def region(kib):
            at = place["at"]
            place["at"] += int(kib * 1024)
            return at

        def sb(name, shape, dt, offset):
            return nc.alloc_sbuf_tensor_at(name, shape, dt, offset=offset)

        def sem(name):
            return ctx.enter_context(nc.semaphore(name))

        x_sb = sb("x_sb", [P, TT, D], F32, region(16))
        act_hl = sb("act_hl", [P, KT, 2 * T], F32R, region(32))
        y_at = region(32)
        xn_T = sb("xn_T", [P, KT, T], F32, y_at)
        xn = sb("xn", [P, TT, D], F32, y_at + 16384)
        attn_hl = sb("attn_hl", [P, PAIRS, 2 * T], F32R, y_at)
        qk_ret = sb("qk_ret", [P, 2 * PAIRS, T], F32, y_at + 16384)
        y_part = sb("y_part", [P, TT, D], F32, y_at + 16384)
        xn2 = sb("xn2", [P, TT, D], F32, y_at)
        hid_hl = sb("hid_hl", [P, KT, 2 * T], F32R, y_at)
        stage = sb("stage", [P, STAGES, G], F32, region(32))
        w_hi = sb("w_hi", [P, 2, G], F32R, region(16))
        w_lo = sb("w_lo", [P, 2, G], F32R, region(16))
        acc = sb("acc", [P, 2, D], F32, region(16))
        ada = sb("ada", [P, 2, D], F32, region(16))
        r_at = region(16)
        q_T = sb("q_T", [P, PAIRS, T], F32, r_at)
        gate = sb("gate", [P, TT, D - ATTN], F32, r_at)
        v_ret = sb("v_ret", [P, TT, D - ATTN], F32, r_at + 8192)
        f_acc = sb("f_acc", [P, TT, D], F32, r_at)
        k_dup = sb("k_dup", [P, 2, T], F32, region(2))
        v_att = sb("v_att", [P, TT, KV_COLS], F32, region(1))
        p_at = region(6)
        probs = sb("probs", [P, 768], F32, p_at)
        probs_T = sb("probs_T", [P, 768], F32, p_at + 3072)
        decay = sb("decay", [P, RET_HEADS, 384], F32, p_at)
        tmp = sb("tmp", [P, 2, T], F32, region(2))
        vec_rows = sb("vec_rows", [64, P], F32, place["at"] - 2048)
        cst = sb("cst", [P, P + 384], F32, region(2))
        ident, dist = cst[:, 0:P], cst[:, P:P + 384]
        ones = sb("ones", [P, P], F32, region(0.5))
        small = sb("small", [P, 352], F32, region(1.375))
        assert place["at"] <= 229368
        vec_T = small[:, 0:64]
        scale1, shift1, scale2, shift2 = (small[:, 64 + 16 * n:80 + 16 * n] for n in range(4))
        sink4 = small[:, 128:160]
        nsink4 = small[:, 160:192]
        sink_row = small[:, 192:208]
        sq_sum = small[:, 208:216]
        rstd = small[:, 216:218]
        mean_sq = small[:, 218:220]
        mx = small[:, 220:224]
        nmax = small[:, 224:228]
        p_sum = small[:, 228:232]
        p_sink = small[:, 232:236]
        p_den = small[:, 236:240]
        p_inv = small[:, 240:244]
        bn6 = small[:, 244:292]
        bn2 = small[:, 292:308]
        gn_rstd = small[:, 308:316]
        d_sink = small[:, 316:320]
        gn_var, gn_std = small[:, 320:328], small[:, 328:336]
        std = small[:, 336:338]

        ps_job = ctx.enter_context(nc.psum_tensor("ps_job", [P, 4, 512], F32))
        ps = ctx.enter_context(nc.psum_tensor("ps", [P, 4, 512], F32))

        vec_loaded, x_loaded, cst_loaded, sinks_loaded = map(sem, ("vec_loaded", "x_loaded", "cst_loaded", "sinks_loaded"))
        decay_loaded, gfin_loaded, out_stored = map(sem, ("decay_loaded", "gfin_loaded", "out_stored"))
        bias_loaded = [sem(f"bias_loaded{n}") for n in range(2)]
        stage_full = [sem(f"stage_full{n}") for n in range(STAGES)]
        ada_full = [sem(f"ada_full{n}") for n in range(2)]
        hi_ready = sem("hi_ready")
        lo_ready = sem("lo_ready")
        group_used = sem("group_used")
        evacuated = sem("evacuated")
        cross_copied = sem("cross_copied")
        acc_zeroed, ada_scaled, ada_used, ones_set, pool_scaled = map(
            sem, ("acc_zeroed", "ada_scaled", "ada_used", "ones_set", "pool_scaled"))
        vec_turned, vec_ready, mod_summed, mod_ready = map(sem, ("vec_turned", "vec_ready", "mod_summed", "mod_ready"))
        squares, normed, turned, turned_out = map(sem, ("squares", "normed", "turned", "turned_out"))
        mod_hi, act_ready = map(sem, ("mod_hi", "act_ready"))
        kv_spread, kv_ready, scaled_keys = map(sem, ("kv_spread", "kv_ready", "scaled_keys"))
        scores_done, logits_ready, exp_done, probs_ready = map(sem, ("scores_done", "logits_ready", "exp_done", "probs_ready"))
        probs_turned, probs_T_ready, pv_done, att_hi, att_ready = map(
            sem, ("probs_turned", "probs_T_ready", "pv_done", "att_hi", "att_ready"))
        qk_done, qk_decayed, gate_exp, ret_done, ret_normed = map(
            sem, ("qk_done", "qk_decayed", "gate_exp", "ret_done", "ret_normed"))
        ret_turned, ret_hi, ret_ready = map(sem, ("ret_turned", "ret_hi", "ret_ready"))
        gate_spread, x_updated, hid_f32, hid_hi, hid_ready, pool_out = map(
            sem, ("gate_spread", "x_updated", "hid_f32", "hid_hi", "hid_ready", "pool_out"))
        vec_step = sem("vec_step")
        out_ready = sem("out_ready")
        var_ready, std_ready = map(sem, ("var_ready", "std_ready"))

        w_in_v = w_in[0].rearrange("(k p) n -> p k n", p=P)
        w_out_v = w_out[0].rearrange("(k p) n -> p k n", p=P)
        w1_v = w1[0].rearrange("(k p) n -> p k n", p=P)
        w2_v = w2[0].rearrange("(k p) n -> p k n", p=P)
        x_v = x[0].rearrange("(t p) n -> p t n", p=P)
        out_v = out[0].rearrange("(t p) n -> p t n", p=P)

        def group_source(j, q):
            kind, c0 = JOBS[j]
            if kind == "feat":
                return w_in_v[:, 8 * q:8 * q + 8, c0:c0 + FEAT_COLS]
            if kind == "tok":
                return w_in_v[:, 4 * q:4 * q + 4, c0:c0 + TOK_COLS]
            k0 = 4 * q + (PAIRS if kind == "out_ret" else 0)
            return w_out_v[:, k0:k0 + 4, c0:c0 + TOK_COLS]

        def ada_before(g):
            return min(48, g - g // 7)

        block = ctx.enter_context(nc.Block())

        @block.sync
        def _(sp):
            for n in range(PRE):
                col, k = FIRST_UNITS[n % 2][0], n // 2
                if n >= STAGES:
                    sp.wait_ge(lo_ready, n - STAGES + 1)
                sp.dma_start(stage[:, n % STAGES, :], w_ada[0, k * P:(k + 1) * P, col:col + D]).then_inc(stage_full[n % STAGES], 16)

            def load_ada(n):
                col = POOL_UNITS[n // KT][0]
                if n >= 2:
                    sp.wait_ge(ada_used, n - 1)
                k = n % KT
                sp.dma_start(ada[:, n % 2, :], w_ada[0, k * P:(k + 1) * P, col:col + D]).then_inc(ada_full[n % 2], 16)

            def load_group(src, slot, read):
                sp.wait_ge(lo_ready, read)
                sp.dma_start(stage[:, slot, :].rearrange("p (k n) -> p k n", k=src.shape[1]), src).then_inc(stage_full[slot], 16)

            for j in range(J_MLP):
                for q in range(N_GROUPS[j]):
                    g = FIRST[j] + q
                    load_group(group_source(j, q), g % STAGES, PRE + g - STAGES + 1)
                    for n in range(ada_before(g), ada_before(g + 1)):
                        load_ada(n)
                    if g == FIRST[J_GR]:
                        sp.wait_ge(pv_done, PAIRS)
                        sp.dma_start(decay[:, :, :], decay_in.rearrange("h p n -> p h n")).then_inc(decay_loaded, 16)

            def w1_groups(row, g0, tile=None):
                for u in range(4):
                    src = w1_v[:, 8 * (u % 2):8 * (u % 2) + 8, bass.ds(row + FEAT_COLS * (u // 2), FEAT_COLS)]
                    g = g0 + u
                    load_group(src, (G_MLP + u) % STAGES, PRE + g - STAGES + 1)
                    if tile is not None:
                        load_ada(tile + u)

            def w1_block(s, g0):
                with sp.Fori(0, F_JOBS // 2) as m:
                    w1_groups(s * D + m * (2 * FEAT_COLS), g0 + m * 4)

            def w2_block(s, g0):
                with sp.Fori(0, STRIPS) as n:
                    for q in range(T_GROUPS):
                        src = w2_v[:, bass.ds(s * KT + 4 * q, 4), bass.ds(n * TOK_COLS, TOK_COLS)]
                        g = g0 + n * T_GROUPS + q
                        load_group(src, (G_MLP + q) % STAGES, PRE + g - STAGES + 1)

            for m in range(F_JOBS // 2):
                w1_groups(m * 2 * FEAT_COLS, G_MLP + 4 * m, 3 * KT + 4 * m)
            with sp.Fori(0, SUPER - 1) as s:
                w2_block(s, G_MLP + 16 + s * 32)
                w1_block(s + 1, G_MLP + 32 + s * 32)
            w2_block(SUPER - 1, G_MLP + 16 + (SUPER - 1) * 32)
            sp.wait_ge(mod_ready, 4)
            sp.dma_start(acc[:, 1, :], g_final.rearrange("(a n) -> a n", a=1).to_broadcast([P, D])).then_inc(gfin_loaded, 16)
            for n in range(2):
                sp.wait_ge(out_ready, n + 1)
                sp.dma_start(out_v[:, 0, n * 1024:(n + 1) * 1024], x_sb[:, 0, n * 1024:(n + 1) * 1024]).then_inc(out_stored, 16)
                sp.wait_ge(pool_out, n + 1)
                sp.dma_start(out_v[:, 1, n * 1024:(n + 1) * 1024], x_sb[:, 1, n * 1024:(n + 1) * 1024]).then_inc(out_stored, 16)
            sp.wait_ge(out_stored, 64)

        @block.gpsimd
        def _(pool):
            zeroed, biased = 0, [0, 0]

            def start_sum(col, a):
                nonlocal zeroed
                nc.gpsimd.memset(acc[:, a, :], 0.0).then_inc(acc_zeroed, 1)
                zeroed += 1
                pool.wait_ge(acc_zeroed, zeroed)
                pool.dma_start(acc[0:1, a, :], b_ada[0:1, col:col + D]).then_inc(bias_loaded[a], 16)
                biased[a] += 1

            for col, a in FIRST_UNITS:
                start_sum(col, a)
            nc.gpsimd.memset(ones[:, :], 1.0).then_inc(ones_set, 1)
            for u, (col, a) in enumerate(POOL_UNITS):
                if col == GT2:
                    pool.wait_ge(gate_spread, STRIPS)
                else:
                    pool.wait_ge(mod_summed, u + 1)
                start_sum(col, a)
                pool.wait_ge(bias_loaded[a], 16 * biased[a])
                for k in range(KT):
                    n = u * KT + k
                    pool.wait_ge(ada_scaled, n + 1)
                    if k:
                        pool.wait_ge(ada_used, n)
                    nc.gpsimd.tensor_tensor(acc[:, a, :], ada[:, n % 2, :], acc[:, a, :], ALU.add).then_inc(ada_used, 1)
            pool.wait_ge(gfin_loaded, 16)
            pool.wait_ge(normed, 3)
            for n in range(2):
                cols = slice(n * 1024, (n + 1) * 1024)
                nc.gpsimd.tensor_scalar(x_sb[:, 1, cols], x_sb[:, 1, cols], rstd[:, 1:2], None, ALU.mult).then_inc(pool_scaled, 1)
                pool.wait_ge(pool_scaled, n + 1)
                nc.gpsimd.tensor_tensor(x_sb[:, 1, cols], x_sb[:, 1, cols], acc[:, 1, cols], ALU.mult).then_inc(pool_out, 1)

        @block.scalar
        def _(act):
            act.dma_start(vec_rows[V_MIX:V_MIX + KT, :], g_mix.rearrange("a (k p) -> (a k) p", p=P)).then_inc(vec_loaded, 16)
            act.dma_start(vec_rows[V_FFN:V_FFN + KT, :], g_ffn.rearrange("a (k p) -> (a k) p", p=P)).then_inc(vec_loaded, 16)
            act.dma_start(vec_rows[V_BETA:V_BETA + 8, :], beta_attn.rearrange("a (k p) -> (a k) p", p=P)).then_inc(vec_loaded, 16)
            act.dma_start(vec_rows[V_GRET:V_GRET + 8, :], g_ret.rearrange("a (k p) -> (a k) p", p=P)).then_inc(vec_loaded, 16)
            act.dma_start(vec_rows[V_C:V_C + KT, :], c.rearrange("a (k p) -> (a k) p", p=P)).then_inc(vec_loaded, 16)
            act.dma_start(cst[:, :], consts).then_inc(cst_loaded, 16)
            act.dma_start(x_sb[:, :, :], x_v).then_inc(x_loaded, 16)
            act.dma_start(sink_row, sinks.to_broadcast([P, 16])).then_inc(sinks_loaded, 16)

            act.wait_ge(x_loaded, 16)
            for t in range(TT):
                nc.scalar.activation(act_hl[:, 4 * t:4 * t + 4, :], x_sb[:, t, :].rearrange("p (k n) -> p k n", k=4), ACT.Square,
                                     accum_out=sq_sum[:, t:t + 1]).then_inc(squares, 1)
            def root(dst, src, n):
                act.wait_ge(var_ready, n)
                nc.scalar.activation(dst, src, ACT.Sqrt).then_inc(std_ready, 1)

            root(std, mean_sq, 1)
            for r in range(8):
                act.wait_ge(turned, r + 1)
                nc.scalar.activation(xn_T[:, 2 * r:2 * r + 2, :], ps[:, r % 4, :].rearrange("p (k n) -> p k n", k=2),
                                     ACT.Copy).then_inc(turned_out, 1)
            act.wait_ge(mod_ready, 2)
            act.wait_ge(turned_out, 8)
            act.wait_ge(squares, 2)
            for k in range(KT):
                nc.scalar.activation(act_hl[:, k, 0:T], xn_T[:, k, :], ACT.Identity, bias=shift1[:, k:k + 1],
                                     scale=scale1[:, k:k + 1]).then_inc(mod_hi, 1)

            def round_group(g, slot, ring, i_fill):
                act.wait_ge(stage_full[slot], 16 * i_fill)
                if not isinstance(g, int) or g >= 2:
                    act.wait_ge(group_used, g - 1)
                nc.scalar.activation(w_hi[:, ring, :], stage[:, slot, :], ACT.Copy).then_inc(hi_ready, 1)

            def static_group(g):
                round_group(g, g % STAGES, g % 2, (PRE + g) // STAGES + 1)

            squared = [TT]

            def row_squares(n, junk):
                act.wait_ge(x_updated, (squared[0] - TT) // TT + 1)
                for t in range(TT):
                    act.wait_ge(squares, squared[0])
                    nc.scalar.activation(junk, x_sb[:, t, n * 512:(n + 1) * 512], ACT.Square,
                                         accum_out=sq_sum[:, 4 * t + n:4 * t + n + 1]).then_inc(squares, 1)
                    squared[0] += 1

            def copy_cross(used, pair):
                act.wait_ge(group_used, used)
                nc.scalar.activation(tmp[:, :, :], ps_job[:, 2 * pair:2 * pair + 2, T:2 * T], ACT.Copy).then_inc(cross_copied, 1)

            def scale_tile(n, slot, k, fill):
                act.wait_ge(ada_full[slot], 16 * fill)
                nc.scalar.activation(ada[:, slot, :], ada[:, slot, :], ACT.Copy, scale=vec_T[:, bass.ds(V_C + k, 1)]).then_inc(ada_scaled, 1)

            def exps(b):
                act.wait_ge(logits_ready, b + 1)
                for t in range(TT):
                    nk, at = key_count(t), 256 * t
                    for e in range(2):
                        s = slice(at + e * nk, at + (e + 1) * nk)
                        i = 2 * t + e
                        nc.scalar.activation(probs[:, s], probs[:, s], ACT.Exp, bias=nmax[:, i:i + 1], accum_out=p_sum[:, i:i + 1]).then_inc(exp_done, 1)
                nc.scalar.activation(p_sink, d_sink, ACT.Exp).then_inc(exp_done, 1)

            def copy_probs_T(b):
                act.wait_ge(probs_turned, b + 1)
                if b:
                    act.wait_ge(pv_done, b)
                nc.scalar.activation(probs_T[:, 256:768], ps[:, 2, :], ACT.Copy).then_inc(probs_T_ready, 1)
                nc.scalar.activation(probs_T[:, 0:256], ps[:, 3, 0:256], ACT.Copy).then_inc(probs_T_ready, 1)

            def attention_head(b):
                act.wait_ge(pv_done, b + 1)
                if b == 0:
                    act.wait_ge(act_ready, KT)
                nc.scalar.activation(attn_hl[:, b, 0:T], ps[:, 3, 256:512], ACT.Copy, scale=vec_T[:, V_BETA + b:V_BETA + b + 1]).then_inc(att_hi, 1)

            def retention_head(h):
                act.wait_ge(ret_turned, h + 1)
                if h == 0:
                    act.wait_ge(group_used, FIRST[J_OA])
                for e in range(2):
                    k = 2 * h + e
                    nc.scalar.activation(act_hl[:, PAIRS + k, 0:T], ps[:, h, e * T:(e + 1) * T], ACT.Copy,
                                         scale=vec_T[:, V_GRET + k:V_GRET + k + 1]).then_inc(ret_hi, 1)

            for j in range(J_MLP):
                for q in range(N_GROUPS[j]):
                    static_group(FIRST[j] + q)
                    for n in range(ada_before(FIRST[j] + q - 1) if j + q else 0, ada_before(FIRST[j] + q)):
                        scale_tile(n, n % 2, n % KT, n // 2 + 1)
                    if q == 0:
                        b = j - J_QKR - 2
                        if 0 <= b < PAIRS:
                            attention_head(b)
                        if j >= 1 and JOBS[j - 1][0] == "feat":
                            if j == 2:
                                act.wait_ge(kv_spread, 2)
                            if j >= 2:
                                act.wait_ge(evacuated, j - 1)
                            copy_cross(FIRST[j], (j - 1) % 2)
                        if j == 1:
                            act.wait_ge(kv_spread, 1)
                            nc.scalar.activation(k_dup[:, :, :], ps[:, 0, :].rearrange("p (k n) -> p k n", k=2), ACT.Copy,
                                                 scale=float(HEAD) ** -0.5).then_inc(scaled_keys, 1)
                        b = j - J_QKR - 1
                        if 0 <= b < PAIRS:
                            exps(b)
                        if JOBS[j - 1][0] == "tok" and J_GR <= j - 1 < J_OA:
                            n = j - 1 - J_GR
                            act.wait_ge(group_used, FIRST[j])
                            pair = (j - 1) % 2
                            if n == 0:
                                act.wait_ge(scores_done, PAIRS)
                            nc.scalar.activation(gate[:, :, n * 512:(n + 1) * 512], ps_job[:, 2 * pair:2 * pair + 2, :], ACT.Exp,
                                                 scale=-1.0).then_inc(gate_exp, 1)
                    if q == 1:
                        b = j - J_QKR - 1
                        if 0 <= b < PAIRS:
                            copy_probs_T(b)
                    if j == J_OA and q == 1:
                        root(gn_std, gn_var, 2)
                    if j == J_OA + 2 and q == 0:
                        retention_head(0)
                    if j == J_OA + 2 and q == 1:
                        retention_head(1)
                    if j == J_OA + 3 and q == 0:
                        retention_head(2)
                    if j == J_OA + 3 and q == 1:
                        retention_head(3)
                    if j > J_OR and q == 1:
                        row_squares(j - 1 - J_OR, v_ret[:, 0, 0:512])
            row_squares(STRIPS - 1, v_ret[:, 0, 0:512])
            root(std, mean_sq, 3)
            assert G_MLP % 2 == 0
            round_group(G_MLP, G_MLP % STAGES, 0, (PRE + G_MLP) // STAGES + 1)
            round_group(G_MLP + 1, (G_MLP + 1) % STAGES, 1, (PRE + G_MLP + 1) // STAGES + 1)
            act.wait_ge(mod_ready, 4)
            act.wait_ge(group_used, G_MLP)
            for k in range(KT):
                if k % 2 == 0:
                    act.wait_ge(turned, 8 + k // 2 + 1)
                nc.scalar.activation(act_hl[:, k, 0:T], ps[:, (k // 2) % 4, (k % 2) * T:(k % 2 + 1) * T], ACT.Identity,
                                     bias=shift2[:, k:k + 1], scale=scale2[:, k:k + 1]).then_inc(mod_hi, 1)

            def fills(g0, u):
                return (PRE + g0 + u) // STAGES + 1

            def hidden_cross(n, used, pair):
                if isinstance(n, int) and n == 0:
                    act.wait_ge(act_ready, 2 * KT)
                else:
                    act.wait_ge(hid_ready, n)
                copy_cross(used, pair)

            def hidden_head(n, k0):
                act.wait_ge(hid_f32, n + 1)
                nc.scalar.activation(hid_hl[:, bass.ds(k0, 2), 0:T], tmp[:, :, :], ACT.Copy).then_inc(hid_hi, 1)

            PB = J_MLP % 2

            def w1_first(n0, g0, fill0, after_w2):
                for u in range(4):
                    if u >= 2 or after_w2:
                        round_group(g0 + u, (G_MLP + u) % STAGES, u % 2, fill0(u))
                    if not after_w2:
                        scale_tile(3 * KT + u, u % 2, u, (3 * KT + u) // 2 + 1)
                    if u == 2:
                        hidden_cross(n0, g0 + 2, PB)
                    if u == 3:
                        hidden_head(n0, 0)

            def w1_rest(n0, g0, fill0, with_ada=False):
                with act.Fori(0, F_JOBS // 2 - 1) as m:
                    for u in range(4):
                        jj, q = u // 2, u % 2
                        round_group(g0 + 4 + u + m * 4, (G_MLP + u) % STAGES, q, fill0(u) + 1 + m)
                        if with_ada:
                            scale_tile(None, q, m * 4 + 4 + u, m * 2 + (3 * KT + 4 + u) // 2 + 1)
                        if q == 0:
                            hidden_cross(n0 + 1 + jj + m * 2, g0 + 4 + 2 * jj + m * 4, (PB + 1 + jj) % 2)
                        else:
                            hidden_head(n0 + 1 + jj + m * 2, m * 4 + 2 + 2 * jj)

            w1_first(0, G_MLP, lambda u: fills(G_MLP, u), False)
            w1_rest(0, G_MLP, lambda u: fills(G_MLP, u), True)

            def w2_block(g0, fill0, n_last, last):
                for jj in range(STRIPS):
                    for q in range(T_GROUPS):
                        u = 4 * jj + q
                        round_group(g0 + u, (G_MLP + u) % STAGES, u % 2, fill0(q) + jj)
                        if jj == 0 and q == 0:
                            hidden_cross(n_last, g0, (PB + 1) % 2)
                        if jj == 0 and q == 1:
                            hidden_head(n_last, KT - 2)
                        if last and jj > 0 and q == 1:
                            row_squares(jj - 1, act_hl[:, 0, :])

            with act.Fori(0, SUPER - 1) as s:
                g0 = G_MLP + 16 + s * 32
                w2_block(g0, lambda q: (PRE + G_MLP + 16 + q) // STAGES + 1 + s * 8, 7 + s * 8, False)
                g1 = G_MLP + 32 + s * 32
                fill1 = lambda u: (PRE + G_MLP + 32 + u) // STAGES + 1 + s * 8
                n1 = 8 + s * 8
                w1_first(n1, g1, fill1, True)
                w1_rest(n1, g1, fill1)
            gl = G_MLP + 16 + 32 * (SUPER - 1)
            w2_block(gl, lambda q: (PRE + gl + q) // STAGES + 1, 8 * SUPER - 1, True)
            row_squares(STRIPS - 1, act_hl[:, 0, :])
            root(std, mean_sq, 4)

        @block.tensor
        def _(pe):
            pe.wait_ge(vec_loaded, 80)
            pe.wait_ge(cst_loaded, 16)
            nc.tensor.transpose(ps[:, 0, 0:64], vec_rows[:, :], ident[0:64, 0:64]).then_inc(vec_turned, 1)

            def turn_normed(src, first):
                for r in range(8):
                    if first and r == 0:
                        pe.wait_ge(vec_ready, 1)
                    if r >= 4:
                        if first:
                            pe.wait_ge(turned_out, r - 3)
                        else:
                            pe.wait_ge(act_ready, KT + 2 * (r - 4) + 2)
                    for e in range(2):
                        for t in range(TT):
                            k = 2 * r + e
                            last = nc.tensor.transpose(ps[:, r % 4, e * T + t * P:e * T + (t + 1) * P], src[:, t, k * P:(k + 1) * P], ident)
                    last.then_inc(turned, 1)

            pe.wait_ge(normed, 1)
            turn_normed(xn, True)

            def sum_mod(a, bank, col):
                for k in range(KT):
                    last = nc.tensor.matmul(ps[:, bank, col + k:col + k + 1], acc[:, a, k * P:(k + 1) * P], ones[:, 0:1], start=True, stop=True)
                last.then_inc(mod_summed, 1)

            pe.wait_ge(ones_set, 1)
            pe.wait_ge(turned_out, 8)
            pe.wait_ge(lo_ready, PRE - 1)
            sum_mod(0, 0, 0)
            pe.wait_ge(lo_ready, PRE)
            sum_mod(1, 1, 0)

            def feature_group(k0, ring, pair, last_group):
                for k in range(8):
                    kt = k0 + k
                    for e in range(2):
                        o = ps_job[:, 2 * pair + e, :]
                        ws = slice(k * FEAT_COLS + e * P, k * FEAT_COLS + (e + 1) * P)
                        nc.tensor.matmul(o, w_hi[:, ring, ws], act_hl[:, kt, :], start=(kt == 0), stop=False)
                        last = nc.tensor.matmul(o[:, T:2 * T], w_lo[:, ring, ws], act_hl[:, kt, 0:T], start=False,
                                                stop=last_group and k == 7)
                last.then_inc(group_used, 1)

            def token_group(src, k0, ring, pair, first_group, last_group):
                for k in range(4):
                    for t in range(TT):
                        o = ps_job[:, 2 * pair + t, :]
                        a_hi = src[:, k0 + k, t * P:(t + 1) * P]
                        a_lo = src[:, k0 + k, T + t * P:T + (t + 1) * P]
                        wh = w_hi[:, ring, k * TOK_COLS:(k + 1) * TOK_COLS]
                        wl = w_lo[:, ring, k * TOK_COLS:(k + 1) * TOK_COLS]
                        nc.tensor.matmul(o, a_hi, wh, start=first_group and k == 0, stop=False)
                        nc.tensor.matmul(o, a_hi, wl, start=False, stop=False)
                        last = nc.tensor.matmul(o, a_lo, wh, start=False, stop=last_group and k == 3)
                last.then_inc(group_used, 1)

            def spread_kv():
                pe.wait_ge(evacuated, 1)
                for e in range(2):
                    for half in range(2):
                        last = nc.tensor.matmul(ps[half * 64:half * 64 + 64, 0, e * T:(e + 1) * T], ident[:, e * 64:e * 64 + 64],
                                                tmp[:, 0, :], start=True, stop=True, skip_group_check=True)
                last.then_inc(kv_spread, 1)
                for t in range(TT):
                    last = nc.tensor.transpose(ps[:, 1, t * P:(t + 1) * P], tmp[:, 1, t * P:(t + 1) * P], ident)
                last.then_inc(kv_spread, 1)

            def scores(b):
                pe.wait_ge(evacuated, J_Q + b // 2 + 1)
                if b == 0:
                    pe.wait_ge(scaled_keys, 1)
                    pe.wait_ge(kv_ready, 1)
                for t in range(TT):
                    nk = key_count(t)
                    for e in range(2):
                        last = nc.tensor.matmul(ps[:, e, P * t:P * t + nk], q_T[64 * e:64 * e + 64, b, t * P:(t + 1) * P],
                                                k_dup[64 * e:64 * e + 64, b // 4, 0:nk], start=True, stop=True)
                last.then_inc(scores_done, 1)

            def turn_probs(b):
                pe.wait_ge(probs_ready, b + 1)
                if b:
                    pe.wait_ge(att_ready, b)
                for e in range(2):
                    for m in range(2):
                        s = slice(256 + e * 256 + m * P, 256 + e * 256 + (m + 1) * P)
                        nc.tensor.transpose(ps[:, 2, e * 256 + m * P:e * 256 + (m + 1) * P], probs[:, s], ident)
                for e in range(2):
                    last = nc.tensor.transpose(ps[:, 3, e * P:(e + 1) * P], probs[:, e * P:(e + 1) * P], ident)
                last.then_inc(probs_turned, 1)

            def probs_values(b):
                pe.wait_ge(probs_T_ready, 2 * b + 2)
                kv = slice(64 * (b // 4), 64 * (b // 4) + 64)
                for e in range(2):
                    o = ps[64 * e:64 * e + 64, 3, 256:512]
                    nc.tensor.matmul(o[:, 0:P], v_att[:, 0, kv], probs_T[:, e * P:(e + 1) * P], start=True, stop=True)
                    for m in range(2):
                        s = slice(256 + e * 256 + m * P, 256 + e * 256 + (m + 1) * P)
                        last = nc.tensor.matmul(o[:, P:2 * P], v_att[:, m, kv], probs_T[:, s], start=(m == 0), stop=(m == 1))
                last.then_inc(pv_done, 1)

            def ret_qk(h):
                for m in range(2):
                    for e in range(2):
                        o = ps[:, h, 0:T] if m == 0 else ps[:, h, T:T + P]
                        last = nc.tensor.matmul(o, qk_ret[:, PAIRS + 2 * h + e, m * P:(m + 1) * P],
                                                qk_ret[:, 2 * h + e, m * P:T], start=(e == 0), stop=(e == 1))
                last.then_inc(qk_done, 1)

            def ret_values(h):
                v = slice(h * RET_HEAD, (h + 1) * RET_HEAD)
                nc.tensor.matmul(ps[:, h, 0:256], decay[:, h, 0:P], v_ret[:, 0, v], start=True, stop=True)
                nc.tensor.matmul(ps[:, h, 256:512], decay[:, h, P:2 * P], v_ret[:, 0, v], start=True, stop=False)
                nc.tensor.matmul(ps[:, h, 256:512], decay[:, h, 2 * P:3 * P], v_ret[:, 1, v], start=False, stop=True).then_inc(ret_done, 1)

            def turn_ret(h):
                pe.wait_ge(ret_normed, h + 1)
                for e in range(2):
                    for t in range(TT):
                        last = nc.tensor.transpose(ps[:, h, e * T + t * P:e * T + (t + 1) * P],
                                                   gate[:, t, (2 * h + e) * P:(2 * h + e + 1) * P], ident)
                last.then_inc(ret_turned, 1)

            def spread_gate(n, bank):
                nc.tensor.matmul(ps[:, bank, :], ones[:, :], acc[:, 0, n * 512:(n + 1) * 512], start=True, stop=True).then_inc(gate_spread, 1)

            for j in range(J_MLP):
                kind = JOBS[j][0]
                for q in range(N_GROUPS[j]):
                    g = FIRST[j] + q
                    pe.wait_ge(lo_ready, PRE + g + 1)
                    if q == 0 and j >= 2:
                        pe.wait_ge(evacuated, j - 1)
                    if j == 0:
                        pe.wait_ge(act_ready, 8 * (q + 1))
                    if j == J_OA and q == 0:
                        pe.wait_ge(att_ready, PAIRS)
                    if j == J_OR:
                        pe.wait_ge(ret_ready, 4 * q + 4)
                    if kind == "feat":
                        feature_group(8 * q, g % 2, j % 2, q == 1)
                    elif kind == "tok":
                        token_group(act_hl, 4 * q, g % 2, j % 2, q == 0, q == 3)
                    elif kind == "out_attn":
                        token_group(attn_hl, 4 * q, g % 2, j % 2, q == 0, q == 1)
                    else:
                        token_group(act_hl, PAIRS + 4 * q, g % 2, j % 2, q == 0, q == 1)
                    b = j - J_QKR
                    if j == 1 and q == 0:
                        spread_kv()
                    if q == 0:
                        if 0 <= b - 1 < PAIRS:
                            turn_probs(b - 1)
                        if 0 <= b < PAIRS:
                            scores(b)
                    if q == 1 and 0 <= b - 1 < PAIRS:
                        probs_values(b - 1)
                    if j == J_GR + 1 and q == 0:
                        pe.wait_ge(att_ready, PAIRS)
                        for h in range(RET_HEADS - 1):
                            ret_qk(h)
                        pe.wait_ge(ada_used, 2 * KT)
                        sum_mod(1, RET_HEADS - 1, 0)
                        pe.wait_ge(mod_ready, 3)
                        ret_qk(RET_HEADS - 1)
                    if j == J_OA and q == 0:
                        pe.wait_ge(qk_decayed, RET_HEADS)
                        for h in range(RET_HEADS):
                            ret_values(h)
                    if j == J_OA + 1 and q == 1:
                        turn_ret(0)
                    if j == J_OA + 2:
                        turn_ret(1 + q)
                    if j == J_OA + 3 and q == 0:
                        turn_ret(3)
                    if j >= J_OR and q == 0:
                        n = j - J_OR
                        if n == 0:
                            pe.wait_ge(ret_ready, 2 * RET_HEADS)
                            pe.wait_ge(ada_used, KT)
                        if n >= 2:
                            pe.wait_ge(x_updated, n - 1)
                        spread_gate(n, n % 2)
                    if j == J_MLP - 1 and q == 0:
                        pe.wait_ge(ada_used, 3 * KT)
                        sum_mod(1, 3, 0)

            pe.wait_ge(normed, 2)
            pe.wait_ge(mod_ready, 4)
            turn_normed(xn2, False)

            PB = J_MLP % 2

            def w1_two(g, j, first):
                for jj in range(2):
                    for q in range(2):
                        u = 2 * jj + q
                        pe.wait_ge(lo_ready, PRE + 1 + u + g)
                        if q == 0:
                            pe.wait_ge(evacuated, j - 1 + jj)
                        if first and jj == 0:
                            pe.wait_ge(act_ready, KT + 8 * (q + 1))
                        feature_group(8 * q, u % 2, (PB + jj) % 2, q == 1)

            def w1_block(g0, j0, first):
                if first:
                    w1_two(g0, j0, True)
                    with pe.Fori(1, F_JOBS // 2) as m:
                        w1_two(g0 + m * 4, j0 + m * 2, False)
                else:
                    with pe.Fori(0, F_JOBS // 2) as m:
                        w1_two(g0 + m * 4, j0 + m * 2, False)

            def w2_block(g0, j0, blocks_done, last):
                for jj in range(STRIPS):
                    for q in range(T_GROUPS):
                        pe.wait_ge(lo_ready, PRE + 1 + 4 * jj + q + g0)
                        if q == 0:
                            pe.wait_ge(evacuated, j0 + jj - 1)
                        if jj == 0 and q == 0:
                            pe.wait_ge(hid_ready, blocks_done - 1)
                        if jj == 0 and q == T_GROUPS - 1:
                            pe.wait_ge(hid_ready, blocks_done)
                        token_group(hid_hl, 4 * q, q % 2, (PB + jj) % 2, q == 0, q == T_GROUPS - 1)
                        if last and q == 0:
                            if jj == 0:
                                pe.wait_ge(ada_used, 4 * KT)
                            if jj >= 2:
                                pe.wait_ge(x_updated, STRIPS + jj - 1)
                            spread_gate(jj, jj % 2)

            w1_block(G_MLP, J_MLP, True)
            with pe.Fori(0, SUPER - 1) as s:
                w2_block(G_MLP + 16 + s * 32, J_MLP + 8 + s * 12, 8 + s * 8, False)
                w1_block(G_MLP + 32 + s * 32, J_MLP + 12 + s * 12, False)
            w2_block(G_MLP + 16 + 32 * (SUPER - 1), J_MLP + 8 + 12 * (SUPER - 1), 8 * SUPER, True)

        @block.vector
        def _(dve):
            steps = [0]

            def link(ins):
                steps[0] += 1
                ins.then_inc(vec_step, 1)
                dve.wait_ge(vec_step, steps[0])

            dve.wait_ge(vec_turned, 1)
            nc.vector.tensor_copy(vec_T, ps[:, 0, 0:64]).then_inc(vec_ready, 1)
            dve.wait_ge(vec_ready, 1)

            def sum_tile(n):
                a, k = n % 2, n // 2
                dve.wait_ge(stage_full[n % STAGES], 16 * (n // STAGES + 1))
                if k:
                    dve.wait_ge(lo_ready, n - 1)
                else:
                    dve.wait_ge(bias_loaded[a], 16)
                nc.vector.scalar_tensor_tensor(out=acc[:, a, :], in0=stage[:, n % STAGES, :], scalar=vec_T[:, V_C + k:V_C + k + 1],
                                               in1=acc[:, a, :], op0=ALU.mult, op1=ALU.add).then_inc(lo_ready, 1)

            def row_norm(total, roots):
                nc.vector.tensor_scalar(mean_sq, total, 1.0 / D, EPS, ALU.mult, ALU.add).then_inc(var_ready, 1)
                dve.wait_ge(std_ready, roots)
                return nc.vector.reciprocal(rstd, std)

            for n in range(PRE):
                sum_tile(n)
                if n == 5:
                    dve.wait_ge(squares, 2)
                    link(row_norm(sq_sum[:, 0:2], 1))
                    for t in range(TT):
                        last = nc.vector.tensor_scalar(xn[:, t, :], x_sb[:, t, :], rstd[:, t:t + 1], None, ALU.mult)
                        if t == 0:
                            link(last)
                    last.then_inc(normed, 1)
                if n == 7:
                    dve.wait_ge(sinks_loaded, 16)
                    s4 = sink4.rearrange("p (b t e) -> p b t e", b=PAIRS, t=2)
                    n4 = nsink4.rearrange("p (b t e) -> p b t e", b=PAIRS, t=2)
                    for t in range(TT):
                        nc.vector.tensor_copy(s4[:, :, t, :], sink_row.rearrange("p (b e) -> p b e", e=2))
                        link(nc.vector.tensor_scalar(n4[:, :, t, :], sink_row.rearrange("p (b e) -> p b e", e=2), -1.0, None, ALU.mult))

            dve.wait_ge(mod_summed, 1)
            nc.vector.scalar_tensor_tensor(out=scale1, in0=ps[:, 0, 0:KT], scalar=1.0, in1=vec_T[:, V_MIX:V_MIX + KT],
                                           op0=ALU.add, op1=ALU.mult).then_inc(mod_ready, 1)
            dve.wait_ge(mod_summed, 2)
            nc.vector.tensor_copy(shift1, ps[:, 1, 0:KT]).then_inc(mod_ready, 1)
            dve.wait_ge(mod_ready, 2)
            dve.wait_ge(turned_out, 8)

            def modulate_tail(source, scale, shift, done):
                for k in range(0, KT, 2):
                    dve.wait_ge(mod_hi, done + k + 2)
                    if k:
                        dve.wait_ge(act_ready, done + k)
                    for e in range(2):
                        w = nc.vector.scalar_tensor_tensor(out=tmp[:, e, :], in0=source(k + e), scalar=scale[:, k + e:k + e + 1],
                                                           in1=act_hl[:, k + e, 0:T].bitcast(F32), op0=ALU.mult, op1=ALU.subtract)
                    link(w)
                    for e in range(2):
                        nc.vector.tensor_scalar(act_hl[:, k + e, T:2 * T], tmp[:, e, :], shift[:, k + e:k + e + 1], None,
                                                ALU.add).then_inc(act_ready, 1)

            def split_group(g, slot, ring, n_hi):
                dve.wait_ge(hi_ready, n_hi)
                if not isinstance(g, int) or g >= 2:
                    dve.wait_ge(group_used, g - 1)
                nc.vector.tensor_tensor(w_lo[:, ring, :], stage[:, slot, :], w_hi[:, ring, :].bitcast(F32), ALU.subtract).then_inc(lo_ready, 1)

            modulate_tail(lambda k: xn_T[:, k, :], scale1, shift1, 0)

            def sum_cross(dst, pair, crossed):
                dve.wait_ge(cross_copied, crossed)
                nc.vector.tensor_tensor(dst, ps_job[:, 2 * pair:2 * pair + 2, 0:T], tmp[:, :, :], ALU.add).then_inc(evacuated, 1)

            def logits(b):
                dve.wait_ge(scores_done, b + 1)
                for t in range(TT):
                    nk, at = key_count(t), 256 * t
                    for e in range(2):
                        h = 2 * b + e
                        slope = 2.0 ** (-8.0 * (h + 1) / (2 * PAIRS))
                        last = nc.vector.scalar_tensor_tensor(out=probs[:, at + e * nk:at + (e + 1) * nk], in0=dist[:, P * t:P * t + nk],
                                                              scalar=float(np.float32(slope)), in1=ps[:, e, P * t:P * t + nk],
                                                              op0=ALU.mult, op1=ALU.add)
                        if (t, e) != (TT - 1, 1):
                            steps[0] += 1
                            last.then_inc(vec_step, 1)
                link(last)
                for t in range(TT):
                    nk, at = key_count(t), 256 * t
                    last = nc.vector.tensor_reduce(mx[:, 2 * t:2 * t + 2], probs[:, at:at + 2 * nk].rearrange("p (e n) -> p e n", e=2), AX_X, ALU.max)
                    if t == 0:
                        steps[0] += 1
                        last.then_inc(vec_step, 1)
                link(last)
                link(nc.vector.scalar_tensor_tensor(out=nmax, in0=mx, scalar=-1.0, in1=nsink4[:, 4 * b:4 * b + 4], op0=ALU.mult, op1=ALU.min))
                nc.vector.tensor_tensor(d_sink, sink4[:, 4 * b:4 * b + 4], nmax, ALU.add).then_inc(logits_ready, 1)

            def normalise(b):
                dve.wait_ge(exp_done, 5 * b + 5)
                link(nc.vector.tensor_tensor(p_den, p_sum, p_sink, ALU.add))
                link(nc.vector.reciprocal(p_inv, p_den))
                for t in range(TT):
                    nk, at = key_count(t), 256 * t
                    for e in range(2):
                        i = 2 * t + e
                        s = slice(at + e * nk, at + (e + 1) * nk)
                        last = nc.vector.tensor_scalar(probs[:, s], probs[:, s], p_inv[:, i:i + 1], None, ALU.mult)
                        if i < 3:
                            steps[0] += 1
                            last.then_inc(vec_step, 1)
                last.then_inc(probs_ready, 1)

            def attention_tail(b):
                dve.wait_ge(att_hi, b + 1)
                nc.vector.scalar_tensor_tensor(out=attn_hl[:, b, T:2 * T], in0=ps[:, 3, 256:512], scalar=vec_T[:, V_BETA + b:V_BETA + b + 1],
                                               in1=attn_hl[:, b, 0:T].bitcast(F32), op0=ALU.mult, op1=ALU.subtract).then_inc(att_ready, 1)

            def silu_gate(n, pair):
                s = gate[:, :, n * 512:(n + 1) * 512]
                dve.wait_ge(gate_exp, n + 1)
                link(nc.vector.tensor_scalar(s, s, 1.0, None, ALU.add))
                link(nc.vector.reciprocal(s, s))
                nc.vector.tensor_tensor(s, ps_job[:, 2 * pair:2 * pair + 2, :], s, ALU.mult).then_inc(evacuated, 1)

            def group_stats():
                for h in range(RET_HEADS):
                    dve.wait_ge(ret_done, h + 1)
                    for t in range(TT):
                        i = 2 * h + t
                        steps[0] += 1
                        nc.vector.bn_stats(bn6[:, 6 * i:6 * i + 6], ps[:, h, t * 256:(t + 1) * 256]).then_inc(vec_step, 1)
                dve.wait_ge(vec_step, steps[0])
                for i in range(2 * RET_HEADS):
                    steps[0] += 1
                    nc.vector.bn_aggr(bn2[:, 2 * i:2 * i + 2], bn6[:, 6 * i:6 * i + 6]).then_inc(vec_step, 1)
                dve.wait_ge(vec_step, steps[0])
                nc.vector.tensor_scalar(gn_var, bn2.rearrange("p (i m) -> p i m", m=2)[:, :, 1], EPS, None, ALU.add).then_inc(var_ready, 1)

            def group_norm(h):
                if h == 0:
                    dve.wait_ge(std_ready, 2)
                    link(nc.vector.reciprocal(gn_rstd, gn_std))
                for t in range(TT):
                    i = 2 * h + t
                    s = gate[:, t, h * RET_HEAD:(h + 1) * RET_HEAD]
                    steps[0] += 1
                    nc.vector.scalar_tensor_tensor(out=s, in0=ps[:, h, t * 256:(t + 1) * 256], scalar=bn2[:, 2 * i:2 * i + 1],
                                                   in1=s, op0=ALU.subtract, op1=ALU.mult).then_inc(vec_step, 1)
                dve.wait_ge(vec_step, steps[0])
                for t in range(TT):
                    i = 2 * h + t
                    s = gate[:, t, h * RET_HEAD:(h + 1) * RET_HEAD]
                    last = nc.vector.tensor_scalar(s, s, gn_rstd[:, i:i + 1], None, ALU.mult)
                    if t == 0:
                        steps[0] += 1
                        last.then_inc(vec_step, 1)
                last.then_inc(ret_normed, 1)

            def retention_tail(h):
                dve.wait_ge(ret_hi, 2 * h + 2)
                for e in range(2):
                    k = 2 * h + e
                    nc.vector.scalar_tensor_tensor(out=act_hl[:, PAIRS + k, T:2 * T], in0=ps[:, h, e * T:(e + 1) * T],
                                                   scalar=vec_T[:, V_GRET + k:V_GRET + k + 1], in1=act_hl[:, PAIRS + k, 0:T].bitcast(F32),
                                                   op0=ALU.mult, op1=ALU.subtract).then_inc(ret_ready, 1)

            def add_residual(part, n, j, pair, used, spread):
                s = slice(n * 512, (n + 1) * 512)
                dve.wait_ge(group_used, used)
                nc.vector.tensor_tensor(part[:, :, s], part[:, :, s], ps_job[:, 2 * pair:2 * pair + 2, :], ALU.add).then_inc(evacuated, 1)
                dve.wait_ge(evacuated, j + 1)
                dve.wait_ge(gate_spread, spread)
                for t in range(TT):
                    link(nc.vector.tensor_tensor(part[:, t, s], part[:, t, s], ps[:, n % 2, :], ALU.mult))
                nc.vector.tensor_tensor(x_sb[:, :, s], x_sb[:, :, s], part[:, :, s], ALU.add).then_inc(x_updated, 1)

            def take_out(j):
                pair, used = j % 2, FIRST[j + 1]
                kind = JOBS[j][0]
                if kind == "feat":
                    if j == 0:
                        dst = tmp[:, :, :]
                    elif j < J_QKR:
                        dst = q_T[:, 2 * (j - J_Q):2 * (j - J_Q) + 2, :]
                    else:
                        dst = qk_ret[:, 2 * (j - J_QKR):2 * (j - J_QKR) + 2, :]
                    sum_cross(dst, pair, j + 1)
                elif kind == "tok" and j < J_GR:
                    n = j - J_VR
                    dve.wait_ge(group_used, used)
                    nc.vector.tensor_copy(v_ret[:, :, n * 512:(n + 1) * 512], ps_job[:, 2 * pair:2 * pair + 2, :]).then_inc(evacuated, 1)
                elif kind == "tok":
                    silu_gate(j - J_GR, pair)
                elif kind == "out_attn":
                    n = j - J_OA
                    dve.wait_ge(group_used, used)
                    nc.vector.tensor_copy(y_part[:, :, n * 512:(n + 1) * 512], ps_job[:, 2 * pair:2 * pair + 2, :]).then_inc(evacuated, 1)
                else:
                    n = j - J_OR
                    add_residual(y_part, n, j, pair, used, n + 1)

            for j in range(J_MLP):
                for q in range(N_GROUPS[j]):
                    g = FIRST[j] + q
                    split_group(g, g % STAGES, g % 2, g + 1)
                    if q == 0:
                        b = j - J_QKR - 2
                        if 0 <= b < PAIRS:
                            attention_tail(b)
                        if j >= 1:
                            take_out(j - 1)
                        if j == 1:
                            dve.wait_ge(kv_spread, 2)
                            nc.vector.tensor_copy(v_att[:, :, :], ps[:, 1, 0:256].rearrange("p (t n) -> p t n", t=2)).then_inc(kv_ready, 1)
                        b = j - J_QKR - 1
                        if 0 <= b < PAIRS:
                            normalise(b)
                    if q == 1:
                        b = j - J_QKR
                        if 0 <= b < PAIRS:
                            logits(b)
                    if j == J_GR + 1 and q == 1:
                        dve.wait_ge(decay_loaded, 16)
                        for h in range(RET_HEADS):
                            if h == RET_HEADS - 1:
                                dve.wait_ge(mod_summed, 3)
                                nc.vector.tensor_copy(shift2, ps[:, h, 0:KT]).then_inc(mod_ready, 1)
                            dve.wait_ge(qk_done, h + 1)
                            nc.vector.tensor_tensor(decay[:, h, :], ps[:, h, 0:384], decay[:, h, :], ALU.mult).then_inc(qk_decayed, 1)
                    if j == J_OA and q == 1:
                        group_stats()
                    if j == J_OA + 1:
                        group_norm(2 * q)
                        group_norm(2 * q + 1)
                    if j == J_OA + 2 and q == 0:
                        retention_tail(0)
                    if j == J_OA + 2 and q == 1:
                        retention_tail(1)
                    if j == J_OA + 3:
                        retention_tail(2 + q)
            take_out(J_MLP - 1)

            dve.wait_ge(squares, 2 + 2 * STRIPS)
            link(nc.vector.tensor_reduce(bn2[:, 0:2], sq_sum.rearrange("p (t n) -> p t n", t=TT), AX_X, ALU.add))
            link(row_norm(bn2[:, 0:2], 3))
            for t in range(TT):
                last = nc.vector.tensor_scalar(xn2[:, t, :], x_sb[:, t, :], rstd[:, t:t + 1], None, ALU.mult)
                if t == 0:
                    link(last)
            last.then_inc(normed, 1)
            dve.wait_ge(mod_summed, 4)
            nc.vector.scalar_tensor_tensor(out=scale2, in0=ps[:, 3, 0:KT], scalar=1.0, in1=vec_T[:, V_FFN:V_FFN + KT],
                                           op0=ALU.add, op1=ALU.mult).then_inc(mod_ready, 1)
            nc.vector.memset(f_acc[:, :, :], 0.0).then_inc(vec_step, 1)
            steps[0] += 1
            split_group(G_MLP, G_MLP % STAGES, 0, G_MLP + 1)
            split_group(G_MLP + 1, (G_MLP + 1) % STAGES, 1, G_MLP + 2)
            dve.wait_ge(mod_ready, 4)
            modulate_tail(lambda k: ps[:, (k // 2) % 4, (k % 2) * T:(k % 2 + 1) * T], scale2, shift2, KT)
            dve.wait_ge(vec_step, steps[0])

            PB = J_MLP % 2

            def hidden(n, crossed, j_done, pair):
                sum_cross(tmp[:, :, :], pair, crossed)
                dve.wait_ge(evacuated, j_done)
                nc.vector.scalar_tensor_tensor(out=tmp[:, :, :], in0=tmp[:, :, :], scalar=0.0, in1=tmp[:, :, :],
                                               op0=ALU.max, op1=ALU.mult).then_inc(hid_f32, 1)

            def hidden_tail(n, k0):
                dve.wait_ge(hid_hi, n + 1)
                nc.vector.tensor_tensor(hid_hl[:, bass.ds(k0, 2), T:2 * T], tmp[:, :, :], hid_hl[:, bass.ds(k0, 2), 0:T].bitcast(F32),
                                        ALU.subtract).then_inc(hid_ready, 1)

            N_FEAT = J_VR

            def add_strip(jj, used, pair):
                s = slice(jj * 512, (jj + 1) * 512)
                dve.wait_ge(group_used, used)
                nc.vector.tensor_tensor(f_acc[:, :, s], f_acc[:, :, s], ps_job[:, 2 * pair:2 * pair + 2, :], ALU.add).then_inc(evacuated, 1)

            def w1_rest(n0, g0, j0):
                with dve.Fori(0, F_JOBS // 2 - 1) as m:
                    for jj in range(2):
                        for q in range(2):
                            u = 2 * jj + q
                            g = g0 + 4 + u + m * 4
                            split_group(g, (G_MLP + u) % STAGES, u % 2, g + 1)
                            n = n0 + 1 + jj + m * 2
                            if q == 0:
                                hidden(n, N_FEAT + 1 + n, j0 + 2 + jj + m * 2, (PB + 1 + jj) % 2)
                            else:
                                hidden_tail(n, m * 4 + 2 + 2 * jj)

            def w1_first(n0, g0, j0, after_w2):
                for u in range(4):
                    if u >= 2 or after_w2:
                        split_group(g0 + u, (G_MLP + u) % STAGES, u % 2, g0 + u + 1)
                    if u == 0 and after_w2:
                        add_strip(STRIPS - 1, g0, (PB + 1) % 2)
                    if u == 2:
                        hidden(n0, N_FEAT + 1 + n0, j0 + 1, PB)
                    if u == 3:
                        hidden_tail(n0, 0)

            def w2_block(g0, j0, n_last, last):
                for jj in range(STRIPS):
                    for q in range(T_GROUPS):
                        u = 4 * jj + q
                        split_group(g0 + u, (G_MLP + u) % STAGES, u % 2, g0 + u + 1)
                        if jj == 0 and q == 0:
                            hidden(n_last, N_FEAT + 1 + n_last, j0, (PB + 1) % 2)
                        if jj == 0 and q == 1:
                            hidden_tail(n_last, KT - 2)
                        if jj > 0 and q == 0:
                            if last:
                                add_residual(f_acc, jj - 1, j0 + jj - 1, (PB + jj - 1) % 2, g0 + 4 * jj, STRIPS + jj)
                            else:
                                add_strip(jj - 1, g0 + 4 * jj, (PB + jj - 1) % 2)

            w1_first(0, G_MLP, J_MLP, False)
            w1_rest(0, G_MLP, J_MLP)
            with dve.Fori(0, SUPER - 1) as s:
                w2_block(G_MLP + 16 + s * 32, J_MLP + 8 + s * 12, 7 + s * 8, False)
                w1_first(8 + s * 8, G_MLP + 32 + s * 32, J_MLP + 12 + s * 12, True)
                w1_rest(8 + s * 8, G_MLP + 32 + s * 32, J_MLP + 12 + s * 12)
            gl, jl = G_MLP + 16 + 32 * (SUPER - 1), J_MLP + 8 + 12 * (SUPER - 1)
            w2_block(gl, jl, 8 * SUPER - 1, True)
            add_residual(f_acc, STRIPS - 1, jl + 3, (PB + 3) % 2, gl + 16, 2 * STRIPS)

            dve.wait_ge(squares, 2 + 4 * STRIPS)
            link(nc.vector.tensor_reduce(bn2[:, 0:2], sq_sum.rearrange("p (t n) -> p t n", t=TT), AX_X, ALU.add))
            row_norm(bn2[:, 0:2], 4).then_inc(normed, 1)
            dve.wait_ge(normed, 3)
            dve.wait_ge(gfin_loaded, 16)
            for n in range(2):
                cols = slice(n * 1024, (n + 1) * 1024)
                nc.vector.scalar_tensor_tensor(out=x_sb[:, 0, cols], in0=x_sb[:, 0, cols], scalar=rstd[:, 0:1],
                                               in1=acc[:, 1, cols], op0=ALU.mult, op1=ALU.mult).then_inc(out_ready, 1)



_INS = ["x", "c", "w_ada", "b_ada", "g_mix", "w_in", "beta_attn", "sinks", "g_ret", "w_out", "g_ffn", "w1", "w2", "g_final"]


def shape_constants():
    tok = np.arange(T)
    consts = np.zeros((P, P + 384), np.float32)
    consts[:, 0:P] = np.eye(P)
    for t in range(TT):
        q = tok[t * P:(t + 1) * P, None]
        k = tok[None, 0:P * (t + 1)]
        behind = q // CHUNK - k // CHUNK
        keep = (behind >= 0) & (behind <= 1)
        consts[:, P + P * t:P + P * t + P * (t + 1)] = np.where(keep, -np.abs(q - k), -1e34)
    log_g = np.log(1.0 - 2.0 ** (-5.0 - np.arange(RET_HEADS, dtype=np.float64)))
    decay = np.zeros((RET_HEADS, P, 384), np.float32)
    k, q = tok[:, None], tok[None, :]
    for h in range(RET_HEADS):
        full = np.where(k // CHUNK <= q // CHUNK, np.exp(log_g[h] * np.abs(q - k)), 0.0) * RET_HEAD ** -0.5
        decay[h, :, 0:T] = full[0:P]
        decay[h, :, T:384] = full[P:T, P:T]
    return consts, decay


def kernel(**inputs):
    import concourse.bacc as _bacc
    from concourse.bass_utils import run_bass_kernel_spmd as _run

    nc = _bacc.Bacc("TRN2", target_bir_lowering=False, num_devices=1)
    arrays = {f"in_{n}": np.ascontiguousarray(inputs[n]) for n in _INS}
    arrays["in_consts"], arrays["in_decay"] = shape_constants()
    args = [nc.dram_tensor(n, a.shape, mybir.dt.from_np(a.dtype), kind="ExternalInput").ap() for n, a in arrays.items()]
    out = nc.dram_tensor("out_y", (1, T, D), F32, kind="ExternalOutput").ap()
    build(nc, *args, out)
    r = _run(nc, [arrays], core_ids=[0])
    return r.results[0]["out_y"]
```

```python
from contextlib import ExitStack

import numpy as np

import concourse.bass as bass
from concourse import mybir

F32 = mybir.dt.float32
F32R = mybir.dt.float32r
ACT = mybir.ActivationFunctionType
ALU = mybir.AluOpType
AX_X = mybir.AxisListType.X

P = 128
D = 2048
T = 256
TT = T // P
KT = D // P
CHUNK = 64
HEAD = 64
KV_COLS = 128
ATTN = D // 2
RET_HEAD = 256
RET_HEADS = (D - ATTN) // RET_HEAD
PAIRS = ATTN // P
FF = 4 * D
EPS = 1e-6
IN_COLS = ATTN + 2 * KV_COLS + 4 * (D - ATTN)
G = 2048
STAGES = 4
FEAT_COLS = 256
TOK_COLS = 512
STRIPS = D // TOK_COLS

Q0 = 0
KV0 = ATTN
QR0 = ATTN + 2 * KV_COLS
KR0 = QR0 + D - ATTN
VR0 = KR0 + D - ATTN
GR0 = VR0 + D - ATTN

JOBS = [("feat", KV0)]
JOBS += [("feat", Q0 + FEAT_COLS * n) for n in range(4)]
JOBS += [("feat", QR0 + FEAT_COLS * n) for n in range(8)]
JOBS += [("tok", GR0 + TOK_COLS * n) for n in range(2)]
JOBS += [("tok", VR0 + TOK_COLS * n) for n in range(2)]
JOBS += [("out_attn", TOK_COLS * n) for n in range(STRIPS)]
JOBS += [("out_ret", TOK_COLS * n) for n in range(STRIPS)]
J_Q, J_QKR, J_GR, J_VR, J_OA, J_OR, J_MLP = 1, 5, 13, 15, 17, 21, 25
N_GROUPS = [4 if kind == "tok" else 2 for kind, _ in JOBS]
FIRST = [sum(N_GROUPS[:j]) for j in range(len(JOBS) + 1)]
SUPER = FF // D
G_MLP = FIRST[J_MLP]
F_JOBS = D // FEAT_COLS
B_GROUPS = 2 * F_JOBS
T_GROUPS = 4

SH1, SC1, GT1, SH2, SC2, GT2 = (n * D for n in range(6))
FIRST_UNITS = [(SC1, 0), (SH1, 1)]
POOL_UNITS = [(GT1, 0), (SH2, 1), (SC2, 1), (GT2, 0)]
PRE = 2 * KT
ADA_WIDE = 40
ADA_BEFORE_MLP = 3 * KT + 2

VEC_PIECES = [(0, 0), (0, 1), (0, 2), (0, 3), (1, 0), (1, 1)]
POOL_PIECES = [(1, 2), (1, 3)]

V_MIX, V_FFN, V_BETA, V_GRET, V_C = 0, 16, 32, 40, 48


def key_count(t):
    return P * (t + 1)


def build(nc, x, c, w_ada, b_ada, g_mix, w_in, beta_attn, sinks, g_ret, w_out, g_ffn, w1, w2,
          g_final, consts, decay_in, out):
    with ExitStack() as ctx:
        base = 16512
        place = {"at": base}

        def region(kib):
            at = place["at"]
            place["at"] += int(kib * 1024)
            return at

        def sb(name, shape, dt, offset):
            return nc.alloc_sbuf_tensor_at(name, shape, dt, offset=offset)

        def sem(name):
            return ctx.enter_context(nc.semaphore(name))

        x_sb = sb("x_sb", [P, TT, D], F32, region(16))
        act_hl = sb("act_hl", [P, KT, 2 * T], F32R, region(32))
        y_at = region(32)
        xn_T = sb("xn_T", [P, KT, T], F32, y_at)
        xn = sb("xn", [P, TT, D], F32, y_at + 16384)
        attn_hl = sb("attn_hl", [P, PAIRS, 2 * T], F32R, y_at)
        qk_ret = sb("qk_ret", [P, 2 * PAIRS, T], F32, y_at + 16384)
        y_part = sb("y_part", [P, TT, D], F32, y_at + 16384)
        xn2 = sb("xn2", [P, TT, D], F32, y_at + 16384)
        h2_T = sb("h2_T", [P, KT, T], F32, y_at)
        hid_hl = sb("hid_hl", [P, KT, 2 * T], F32R, y_at)
        stage = sb("stage", [P, STAGES, G], F32, region(32))
        w_hi = sb("w_hi", [P, 2, G], F32R, region(16))
        w_lo = sb("w_lo", [P, 2, G], F32R, region(16))
        acc = sb("acc", [P, 2, D], F32, region(16))
        ada = sb("ada", [P, 2, D], F32, region(16))
        r_at = region(16)
        q_T = sb("q_T", [P, PAIRS, T], F32, r_at)
        gate = sb("gate", [P, TT, D - ATTN], F32, r_at)
        v_ret = sb("v_ret", [P, TT, D - ATTN], F32, r_at + 8192)
        f_acc = sb("f_acc", [P, TT, D], F32, r_at)
        k_dup = sb("k_dup", [P, 2, T], F32, region(2))
        v_att = sb("v_att", [P, TT, KV_COLS], F32, region(1))
        p_at = region(6)
        probs = [sb("probs_even", [P, 768], F32, p_at), sb("probs_odd", [P, 768], F32, r_at + 8192)]
        probs_T = sb("probs_T", [P, 768], F32, p_at + 3072)
        decay = sb("decay", [P, RET_HEADS, 384], F32, p_at)
        tmp = sb("tmp", [P, 2, T], F32, region(2))
        vec_rows = sb("vec_rows", [64, P], F32, place["at"] - 2048)
        cst = sb("cst", [P, P + 384], F32, region(2))
        ident, dist = cst[:, 0:P], cst[:, P:P + 384]
        ones = sb("ones", [P, P], F32, region(0.5))
        small = sb("small", [P, 352], F32, region(1.375))
        assert place["at"] <= 229368
        vec_T = small[:, 0:64]
        scale1, shift1, scale2, shift2 = (small[:, 64 + 16 * n:80 + 16 * n] for n in range(4))
        sink4 = small[:, 128:160]
        nsink4 = small[:, 160:192]
        sink_row = small[:, 192:208]
        sq_sum = small[:, 208:216]
        rstd = small[:, 216:218]
        mean_sq = small[:, 218:220]
        mx = small[:, 220:224]
        nmax = small[:, 224:228]
        p_sum = small[:, 228:232]
        p_sink = small[:, 232:236]
        p_den = small[:, 236:240]
        p_inv = small[:, 240:244]
        bn6 = small[:, 244:292]
        bn2 = small[:, 292:308]
        gn_rstd = small[:, 308:316]
        d_sink = small[:, 316:320]
        gn_var, gn_std = small[:, 320:328], small[:, 328:336]
        std = small[:, 336:338]
        newton = small[:, 338:346]

        ps_job = ctx.enter_context(nc.psum_tensor("ps_job", [P, 4, 512], F32))
        ps = ctx.enter_context(nc.psum_tensor("ps", [P, 4, 512], F32))

        vec_loaded, x_loaded, cst_loaded, sinks_loaded = map(sem, ("vec_loaded", "x_loaded", "cst_loaded", "sinks_loaded"))
        decay_loaded, gfin_loaded, out_stored = map(sem, ("decay_loaded", "gfin_loaded", "out_stored"))
        bias_loaded = [sem(f"bias_loaded{n}") for n in range(2)]
        stage_full = [sem(f"stage_full{n}") for n in range(STAGES)]
        ada_full = [sem(f"ada_full{n}") for n in range(4)]
        hi_ready = sem("hi_ready")
        lo_ready = sem("lo_ready")
        group_used = sem("group_used")
        evacuated = sem("evacuated")
        cross_copied = sem("cross_copied")
        acc_zeroed, ada_scaled, ada_used, ones_set, act_scaled = map(
            sem, ("acc_zeroed", "ada_scaled", "ada_used", "ones_set", "act_scaled"))
        vec_turned, vec_ready, mod_summed, mod_ready = map(sem, ("vec_turned", "vec_ready", "mod_summed", "mod_ready"))
        squares, normed, turned, turned_out = map(sem, ("squares", "normed", "turned", "turned_out"))
        h_ready, mod_hi, act_ready = map(sem, ("h_ready", "mod_hi", "act_ready"))
        kv_spread, kv_ready, scaled_keys = map(sem, ("kv_spread", "kv_ready", "scaled_keys"))
        scores_done, logits_ready, exp_done, probs_ready = map(sem, ("scores_done", "logits_ready", "exp_done", "probs_ready"))
        probs_turned, probs_T_ready, pv_done, att_hi, att_ready = map(
            sem, ("probs_turned", "probs_T_ready", "pv_done", "att_hi", "att_ready"))
        qk_done, qk_decayed, gate_exp, ret_done, ret_normed = map(
            sem, ("qk_done", "qk_decayed", "gate_exp", "ret_done", "ret_normed"))
        ret_turned, ret_hi, ret_ready = map(sem, ("ret_turned", "ret_hi", "ret_ready"))
        gate_spread, gate_copied, x_updated, hid_f32, hid_hi, hid_ready, pool_out = map(
            sem, ("gate_spread", "gate_copied", "x_updated", "hid_f32", "hid_hi", "hid_ready", "pool_out"))
        vec_step = sem("vec_step")
        out_ready = sem("out_ready")
        x_reloaded = sem("x_reloaded")
        f_zeroed = sem("f_zeroed")
        var_ready, std_ready = map(sem, ("var_ready", "std_ready"))

        w_in_v = w_in[0].rearrange("(k p) n -> p k n", p=P)
        w_out_v = w_out[0].rearrange("(k p) n -> p k n", p=P)
        w1_v = w1[0].rearrange("(k p) n -> p k n", p=P)
        w2_v = w2[0].rearrange("(k p) n -> p k n", p=P)
        x_v = x[0].rearrange("(t p) n -> p t n", p=P)
        out_v = out[0].rearrange("(t p) n -> p t n", p=P)

        def group_source(j, q):
            kind, c0 = JOBS[j]
            if kind == "feat":
                return w_in_v[:, 8 * q:8 * q + 8, c0:c0 + FEAT_COLS]
            if kind == "tok":
                return w_in_v[:, 4 * q:4 * q + 4, c0:c0 + TOK_COLS]
            k0 = 4 * q + (PAIRS if kind == "out_ret" else 0)
            return w_out_v[:, k0:k0 + 4, c0:c0 + TOK_COLS]

        def ada_before(g):
            if g <= ADA_WIDE:
                return g
            return min(ADA_BEFORE_MLP, ADA_WIDE + (g - ADA_WIDE) * 2 // 3)

        def pair_at(g, step):
            b, odd = divmod(g - step - FIRST[J_QKR], 2)
            return b if not odd and 0 <= b < PAIRS else None

        ada_slots = [ada[:, 0, :], ada[:, 1, :], x_sb[:, 0, :], x_sb[:, 1, :]]

        def ada_slot(n):
            return n % 4 if n < ADA_WIDE else n % 2

        def ada_fill(n):
            return n // 4 + 1 if n < ADA_WIDE else ADA_WIDE // 4 + (n - ADA_WIDE) // 2 + 1

        block = ctx.enter_context(nc.Block())

        @block.sync
        def _(sp):
            for n in range(PRE):
                col, k = FIRST_UNITS[n % 2][0], n // 2
                if n >= STAGES:
                    sp.wait_ge(lo_ready, n - STAGES + 1)
                sp.dma_start(stage[:, n % STAGES, :], w_ada[0, k * P:(k + 1) * P, col:col + D]).then_inc(stage_full[n % STAGES], 16)

            def load_group(src, slot, read):
                sp.wait_ge(lo_ready, read)
                sp.dma_start(stage[:, slot, :].rearrange("p (k n) -> p k n", k=src.shape[1]), src).then_inc(stage_full[slot], 16)

            for j in range(J_MLP):
                for q in range(N_GROUPS[j]):
                    g = FIRST[j] + q
                    load_group(group_source(j, q), g % STAGES, PRE + g - STAGES + 1)
                    if g == FIRST[J_VR]:
                        sp.wait_ge(pv_done, PAIRS)
                        sp.dma_start(decay[:, :, :], decay_in.rearrange("h p n -> p h n")).then_inc(decay_loaded, 16)

            def w1_groups(row, g0):
                for u in range(4):
                    src = w1_v[:, 8 * (u % 2):8 * (u % 2) + 8, bass.ds(row + FEAT_COLS * (u // 2), FEAT_COLS)]
                    g = g0 + u
                    load_group(src, (G_MLP + u) % STAGES, PRE + g - STAGES + 1)

            def w1_block(s, g0):
                with sp.Fori(0, F_JOBS // 2) as m:
                    w1_groups(s * D + m * (2 * FEAT_COLS), g0 + m * 4)

            def w2_block(s, g0):
                with sp.Fori(0, STRIPS) as n:
                    for q in range(T_GROUPS):
                        src = w2_v[:, bass.ds(s * KT + 4 * q, 4), bass.ds(n * TOK_COLS, TOK_COLS)]
                        g = g0 + n * T_GROUPS + q
                        load_group(src, (G_MLP + q) % STAGES, PRE + g - STAGES + 1)

            w1_block(0, G_MLP)
            with sp.Fori(0, SUPER - 1) as s:
                w2_block(s, G_MLP + 16 + s * 32)
                w1_block(s + 1, G_MLP + 32 + s * 32)
            w2_block(SUPER - 1, G_MLP + 16 + (SUPER - 1) * 32)
            sp.wait_ge(mod_ready, 4)
            sp.dma_start(acc[:, 1, :], g_final.rearrange("(a n) -> a n", a=1).to_broadcast([P, D])).then_inc(gfin_loaded, 16)
            def store(t, n):
                sp.dma_start(out_v[:, t, n * TOK_COLS:(n + 1) * TOK_COLS], x_sb[:, t, n * TOK_COLS:(n + 1) * TOK_COLS]).then_inc(out_stored, 16)

            for i, (t, n) in enumerate(VEC_PIECES):
                sp.wait_ge(out_ready, i + 1)
                store(t, n)
                if i % 3 == 2:
                    sp.wait_ge(pool_out, i // 3 + 1)
                    store(*POOL_PIECES[i // 3])
            sp.wait_ge(out_stored, 16 * TT * STRIPS)

        @block.gpsimd
        def _(pool):
            zeroed, biased = 0, [0, 0]

            def start_sum(col, a):
                nonlocal zeroed
                nc.gpsimd.memset(acc[:, a, :], 0.0).then_inc(acc_zeroed, 1)
                zeroed += 1
                pool.wait_ge(acc_zeroed, zeroed)
                pool.dma_start(acc[0:1, a, :], b_ada[0:1, col:col + D]).then_inc(bias_loaded[a], 16)
                biased[a] += 1

            for col, a in FIRST_UNITS:
                start_sum(col, a)
            nc.gpsimd.memset(ones[:, :], 1.0).then_inc(ones_set, 1)

            def load_tile(n):
                u, k = n // KT, n % KT
                col = POOL_UNITS[u][0]
                pool.dma_start(ada_slots[ada_slot(n)], w_ada[0, k * P:(k + 1) * P, col:col + D]).then_inc(ada_full[ada_slot(n)], 16)

            pool.wait_ge(lo_ready, PRE - STAGES)
            load_tile(0)
            load_tile(1)
            pool.wait_ge(normed, 1)
            load_tile(2)
            load_tile(3)
            for u, (col, a) in enumerate(POOL_UNITS):
                if col == GT2:
                    pool.wait_ge(gate_spread, STRIPS)
                else:
                    pool.wait_ge(mod_summed, u + 1)
                start_sum(col, a)
                pool.wait_ge(bias_loaded[a], 16 * biased[a])
                for k in range(KT):
                    n = u * KT + k
                    pool.wait_ge(ada_scaled, n + 1)
                    nc.gpsimd.tensor_tensor(acc[:, a, :], ada_slots[ada_slot(n)], acc[:, a, :], ALU.add).then_inc(ada_used, 1)
                    pool.wait_ge(ada_used, n + 1)
                    if n < ADA_WIDE - 2:
                        load_tile(n + 4)
                    elif n == ADA_WIDE - 1:
                        pool.dma_start(x_sb[:, :, :], x_v).then_inc(x_reloaded, 16)
                    elif ADA_WIDE <= n < KT * len(POOL_UNITS) - 2:
                        load_tile(n + 2)
                    if n == 3 * KT + 3:
                        pool.wait_ge(squares, 2 + 2 * STRIPS)
                        nc.gpsimd.memset(f_acc[:, :, :], 0.0).then_inc(f_zeroed, 1)
            pool.wait_ge(gfin_loaded, 16)
            for i, (t, n) in enumerate(POOL_PIECES):
                cols = slice(n * TOK_COLS, (n + 1) * TOK_COLS)
                pool.wait_ge(act_scaled, i + 1)
                nc.gpsimd.tensor_tensor(x_sb[:, t, cols], x_sb[:, t, cols], acc[:, 1, cols], ALU.mult).then_inc(pool_out, 1)

        @block.scalar
        def _(act):
            act.dma_start(vec_rows[V_MIX:V_MIX + KT, :], g_mix.rearrange("a (k p) -> (a k) p", p=P)).then_inc(vec_loaded, 16)
            act.dma_start(vec_rows[V_FFN:V_FFN + KT, :], g_ffn.rearrange("a (k p) -> (a k) p", p=P)).then_inc(vec_loaded, 16)
            act.dma_start(vec_rows[V_BETA:V_BETA + 8, :], beta_attn.rearrange("a (k p) -> (a k) p", p=P)).then_inc(vec_loaded, 16)
            act.dma_start(vec_rows[V_GRET:V_GRET + 8, :], g_ret.rearrange("a (k p) -> (a k) p", p=P)).then_inc(vec_loaded, 16)
            act.dma_start(vec_rows[V_C:V_C + KT, :], c.rearrange("a (k p) -> (a k) p", p=P)).then_inc(vec_loaded, 16)
            act.dma_start(cst[:, :], consts).then_inc(cst_loaded, 16)
            act.dma_start(x_sb[:, :, :], x_v).then_inc(x_loaded, 16)
            act.dma_start(sink_row, sinks.to_broadcast([P, 16])).then_inc(sinks_loaded, 16)

            act.wait_ge(x_loaded, 16)
            for t in range(TT):
                nc.scalar.activation(act_hl[:, 4 * t:4 * t + 4, :], x_sb[:, t, :].rearrange("p (k n) -> p k n", k=4), ACT.Square,
                                     accum_out=sq_sum[:, t:t + 1]).then_inc(squares, 1)
            def root(dst, src, n):
                act.wait_ge(var_ready, n)
                nc.scalar.activation(dst, src, ACT.Sqrt).then_inc(std_ready, 1)

            root(std, mean_sq, 1)
            for r in range(8):
                act.wait_ge(turned, r + 1)
                nc.scalar.activation(xn_T[:, 2 * r:2 * r + 2, :], ps[:, r % 4, :].rearrange("p (k n) -> p k n", k=2),
                                     ACT.Copy).then_inc(turned_out, 1)
            def round_group(g, slot, ring, i_fill):
                act.wait_ge(stage_full[slot], 16 * i_fill)
                if not isinstance(g, int) or g >= 2:
                    act.wait_ge(group_used, g - 1)
                nc.scalar.activation(w_hi[:, ring, :], stage[:, slot, :], ACT.Copy).then_inc(hi_ready, 1)

            def static_group(g):
                round_group(g, g % STAGES, g % 2, (PRE + g) // STAGES + 1)

            static_group(0)
            for q in range(4):
                act.wait_ge(h_ready, 4 * q + 4)
                if q == 0:
                    act.wait_ge(squares, 2)
                nc.scalar.activation(act_hl[:, 4 * q:4 * q + 4, 0:T], xn_T[:, 4 * q:4 * q + 4, :], ACT.Copy).then_inc(mod_hi, 1)
            static_group(1)

            def copy_gate(n, spread):
                act.wait_ge(gate_spread, spread)
                if spread > 1:
                    act.wait_ge(x_updated, spread - 1)
                nc.scalar.activation(tmp.rearrange("p a n -> p (a n)"), ps[:, n % 2, :], ACT.Copy).then_inc(gate_copied, 1)

            squared = [TT]

            def row_squares(n, junk):
                act.wait_ge(x_updated, (squared[0] - TT) // TT + 1)
                for t in range(TT):
                    act.wait_ge(squares, squared[0])
                    nc.scalar.activation(junk, x_sb[:, t, n * 512:(n + 1) * 512], ACT.Square,
                                         accum_out=sq_sum[:, 4 * t + n:4 * t + n + 1]).then_inc(squares, 1)
                    squared[0] += 1

            def copy_cross(used, pair):
                act.wait_ge(group_used, used)
                nc.scalar.activation(tmp[:, :, :], ps_job[:, 2 * pair:2 * pair + 2, T:2 * T], ACT.Copy).then_inc(cross_copied, 1)

            def scale_tile(slot, k, fill):
                act.wait_ge(ada_full[slot], 16 * fill)
                nc.scalar.activation(ada_slots[slot], ada_slots[slot], ACT.Copy, scale=vec_T[:, bass.ds(V_C + k, 1)]).then_inc(ada_scaled, 1)

            def exps(b):
                act.wait_ge(logits_ready, b + 1)
                for t in range(TT):
                    nk, at = key_count(t), 256 * t
                    for e in range(2):
                        s = slice(at + e * nk, at + (e + 1) * nk)
                        i = 2 * t + e
                        nc.scalar.activation(probs[b % 2][:, s], probs[b % 2][:, s], ACT.Exp, bias=nmax[:, i:i + 1], accum_out=p_sum[:, i:i + 1]).then_inc(exp_done, 1)
                nc.scalar.activation(p_sink, d_sink, ACT.Exp).then_inc(exp_done, 1)

            def copy_probs_T(b):
                act.wait_ge(probs_turned, b + 1)
                if b:
                    act.wait_ge(pv_done, b)
                nc.scalar.activation(probs_T[:, 256:768], ps[:, 2, :], ACT.Copy).then_inc(probs_T_ready, 1)
                nc.scalar.activation(probs_T[:, 0:256], ps[:, 3, 0:256], ACT.Copy).then_inc(probs_T_ready, 1)

            def attention_head(b):
                act.wait_ge(pv_done, b + 1)
                if b == 0:
                    act.wait_ge(act_ready, 4)
                nc.scalar.activation(attn_hl[:, b, 0:T], ps[:, 3, 256:512], ACT.Copy, scale=vec_T[:, V_BETA + b:V_BETA + b + 1]).then_inc(att_hi, 1)

            def retention_head(h):
                act.wait_ge(ret_turned, h + 1)
                if h == 0:
                    act.wait_ge(group_used, FIRST[J_OA])
                for e in range(2):
                    k = 2 * h + e
                    nc.scalar.activation(act_hl[:, PAIRS + k, 0:T], ps[:, h, e * T:(e + 1) * T], ACT.Copy,
                                         scale=vec_T[:, V_GRET + k:V_GRET + k + 1]).then_inc(ret_hi, 1)

            for j in range(J_MLP):
                for q in range(N_GROUPS[j]):
                    g = FIRST[j] + q
                    if g >= 2:
                        static_group(g)
                    if q == 1 and j >= 1 and JOBS[j - 1][0] == "feat":
                        if j == 2:
                            act.wait_ge(kv_spread, 2)
                        if j >= 2:
                            act.wait_ge(evacuated, j - 1)
                        copy_cross(FIRST[j], (j - 1) % 2)
                    if j == 2 and q == 1:
                        act.wait_ge(kv_spread, 1)
                        nc.scalar.activation(k_dup[:, :, :], ps[:, 0, :].rearrange("p (k n) -> p k n", k=2), ACT.Copy,
                                             scale=float(HEAD) ** -0.5).then_inc(scaled_keys, 1)
                    if pair_at(g, 8) is not None:
                        attention_head(pair_at(g, 8))
                    if pair_at(g, 4) is not None:
                        exps(pair_at(g, 4))
                    if pair_at(g, 7) is not None:
                        copy_probs_T(pair_at(g, 7))
                    if q == 1 and J_GR <= j - 1 < J_VR:
                        n = j - 1 - J_GR
                        act.wait_ge(group_used, FIRST[j])
                        pair = (j - 1) % 2
                        if n == 0:
                            act.wait_ge(scores_done, PAIRS)
                        nc.scalar.activation(gate[:, :, n * 512:(n + 1) * 512], ps_job[:, 2 * pair:2 * pair + 2, :], ACT.Exp,
                                             scale=-1.0).then_inc(gate_exp, 1)
                    if g == FIRST[J_OA] + 4:
                        root(gn_std, gn_var, 2)
                    if g in (FIRST[J_OA] + 6, FIRST[J_OA] + 7):
                        retention_head(2 * (g - FIRST[J_OA] - 6))
                        retention_head(2 * (g - FIRST[J_OA] - 6) + 1)
                    if j > J_OR and q == 1:
                        row_squares(j - 1 - J_OR, v_ret[:, 0, 0:512])
                    if j >= J_OR and q == 1:
                        copy_gate(j - J_OR, j - J_OR + 1)
                    for n in range(ada_before(g - 1) if g else 0, ada_before(g)):
                        scale_tile(ada_slot(n), n % KT, ada_fill(n))
            static_group(G_MLP)
            row_squares(STRIPS - 1, v_ret[:, 0, 0:512])
            root(std, mean_sq, 3)
            static_group(G_MLP + 1)
            act.wait_ge(mod_ready, 4)
            for k in range(KT):
                if k % 2 == 0:
                    act.wait_ge(turned, 8 + k // 2 + 1)
                nc.scalar.activation(h2_T[:, k, :], ps[:, (k // 2) % 4, (k % 2) * T:(k % 2 + 1) * T], ACT.Identity,
                                     bias=shift2[:, k:k + 1], scale=scale2[:, k:k + 1]).then_inc(h_ready, 1)

            def fills(g0, u):
                return (PRE + g0 + u) // STAGES + 1

            def hidden_cross(n, used, pair):
                if isinstance(n, int) and n == 0:
                    act.wait_ge(x_updated, STRIPS)
                else:
                    act.wait_ge(hid_ready, n)
                copy_cross(used, pair)

            def hidden_head(n, k0):
                act.wait_ge(hid_f32, n + 1)
                nc.scalar.activation(hid_hl[:, bass.ds(k0, 2), 0:T], tmp[:, :, :], ACT.Copy).then_inc(hid_hi, 1)

            PB = J_MLP % 2

            def w1_first(n0, g0, fill0, after_w2):
                for u in range(4):
                    if u >= 2 or after_w2:
                        round_group(g0 + u, (G_MLP + u) % STAGES, u % 2, fill0(u))
                    if not after_w2 and u >= 2:
                        scale_tile(u % 2, u, ada_fill(3 * KT + u))
                    if u == 2:
                        hidden_cross(n0, g0 + 2, PB)
                    if u == 3:
                        hidden_head(n0, 0)

            def w1_rest(n0, g0, fill0):
                with act.Fori(0, F_JOBS // 2 - 1) as m:
                    for u in range(4):
                        jj, q = u // 2, u % 2
                        round_group(g0 + 4 + u + m * 4, (G_MLP + u) % STAGES, q, fill0(u) + 1 + m)
                        if q == 0:
                            hidden_cross(n0 + 1 + jj + m * 2, g0 + 4 + 2 * jj + m * 4, (PB + 1 + jj) % 2)
                        else:
                            hidden_head(n0 + 1 + jj + m * 2, m * 4 + 2 + 2 * jj)

            w1_first(0, G_MLP, lambda u: fills(G_MLP, u), False)
            w1_rest(0, G_MLP, lambda u: fills(G_MLP, u))

            def w2_block(g0, fill0, n_last, last, s=None):
                for jj in range(STRIPS):
                    for q in range(T_GROUPS):
                        u = 4 * jj + q
                        round_group(g0 + u, (G_MLP + u) % STAGES, u % 2, fill0(q) + jj)
                        if jj == 0 and q == 0:
                            hidden_cross(n_last, g0, (PB + 1) % 2)
                        if jj == 0 and q == 1:
                            hidden_head(n_last, KT - 2)
                        if not last and q == 1:
                            scale_tile(jj % 2, s * 4 + 4 + jj, s * 2 + ada_fill(3 * KT + 4 + jj))
                        if last and jj > 0 and q == 1:
                            row_squares(jj - 1, act_hl[:, 0, :])
                        if last and q == 2:
                            if jj == 0:
                                act.wait_ge(hid_ready, n_last + 1)
                            copy_gate(jj, STRIPS + jj + 1)

            with act.Fori(0, SUPER - 1) as s:
                g0 = G_MLP + 16 + s * 32
                w2_block(g0, lambda q: (PRE + G_MLP + 16 + q) // STAGES + 1 + s * 8, 7 + s * 8, False, s)
                g1 = G_MLP + 32 + s * 32
                fill1 = lambda u: (PRE + G_MLP + 32 + u) // STAGES + 1 + s * 8
                n1 = 8 + s * 8
                w1_first(n1, g1, fill1, True)
                w1_rest(n1, g1, fill1)
            gl = G_MLP + 16 + 32 * (SUPER - 1)
            w2_block(gl, lambda q: (PRE + gl + q) // STAGES + 1, 8 * SUPER - 1, True)
            row_squares(STRIPS - 1, act_hl[:, 0, :])
            root(std, mean_sq, 4)
            act.wait_ge(normed, 2 + STRIPS)
            for t, n in POOL_PIECES:
                cols = slice(n * TOK_COLS, (n + 1) * TOK_COLS)
                nc.scalar.activation(x_sb[:, t, cols], x_sb[:, t, cols], ACT.Copy, scale=rstd[:, t:t + 1]).then_inc(act_scaled, 1)

        @block.tensor
        def _(pe):
            pe.wait_ge(vec_loaded, 80)
            pe.wait_ge(cst_loaded, 16)
            nc.tensor.transpose(ps[:, 0, 0:64], vec_rows[:, :], ident[0:64, 0:64]).then_inc(vec_turned, 1)

            def turn_normed(src, first):
                for r in range(8):
                    if first and r == 0:
                        pe.wait_ge(vec_ready, 1)
                    if not first and r % 2 == 0:
                        pe.wait_ge(normed, 2 + r // 2)
                    if r >= 4 and first:
                        pe.wait_ge(turned_out, r - 3)
                    elif r >= 4:
                        pe.wait_ge(h_ready, KT + 2 * (r - 4) + 2)
                    for e in range(2):
                        for t in range(TT):
                            k = 2 * r + e
                            last = nc.tensor.transpose(ps[:, r % 4, e * T + t * P:e * T + (t + 1) * P], src[:, t, k * P:(k + 1) * P], ident)
                    last.then_inc(turned, 1)

            pe.wait_ge(normed, 1)
            turn_normed(xn, True)

            def sum_mod(a, bank, col):
                for k in range(KT):
                    last = nc.tensor.matmul(ps[:, bank, col + k:col + k + 1], acc[:, a, k * P:(k + 1) * P], ones[:, 0:1], start=True, stop=True)
                last.then_inc(mod_summed, 1)

            pe.wait_ge(ones_set, 1)
            pe.wait_ge(turned_out, 8)
            pe.wait_ge(lo_ready, PRE - 1)
            sum_mod(0, 0, 0)
            pe.wait_ge(lo_ready, PRE)
            sum_mod(1, 1, 0)

            def feature_group(k0, ring, pair, last_group):
                for k in range(8):
                    kt = k0 + k
                    for e in range(2):
                        o = ps_job[:, 2 * pair + e, :]
                        ws = slice(k * FEAT_COLS + e * P, k * FEAT_COLS + (e + 1) * P)
                        nc.tensor.matmul(o, w_hi[:, ring, ws], act_hl[:, kt, :], start=(kt == 0), stop=False)
                        last = nc.tensor.matmul(o[:, T:2 * T], w_lo[:, ring, ws], act_hl[:, kt, 0:T], start=False,
                                                stop=last_group and k == 7)
                last.then_inc(group_used, 1)

            def token_group(src, k0, ring, pair, first_group, last_group):
                for k in range(4):
                    for t in range(TT):
                        o = ps_job[:, 2 * pair + t, :]
                        a_hi = src[:, k0 + k, t * P:(t + 1) * P]
                        a_lo = src[:, k0 + k, T + t * P:T + (t + 1) * P]
                        wh = w_hi[:, ring, k * TOK_COLS:(k + 1) * TOK_COLS]
                        wl = w_lo[:, ring, k * TOK_COLS:(k + 1) * TOK_COLS]
                        nc.tensor.matmul(o, a_hi, wh, start=first_group and k == 0, stop=False)
                        nc.tensor.matmul(o, a_hi, wl, start=False, stop=False)
                        last = nc.tensor.matmul(o, a_lo, wh, start=False, stop=last_group and k == 3)
                last.then_inc(group_used, 1)

            def spread_kv():
                pe.wait_ge(evacuated, 1)
                for e in range(2):
                    for half in range(2):
                        last = nc.tensor.matmul(ps[half * 64:half * 64 + 64, 0, e * T:(e + 1) * T], ident[:, e * 64:e * 64 + 64],
                                                tmp[:, 0, :], start=True, stop=True, skip_group_check=True)
                last.then_inc(kv_spread, 1)
                for t in range(TT):
                    last = nc.tensor.transpose(ps[:, 1, t * P:(t + 1) * P], tmp[:, 1, t * P:(t + 1) * P], ident)
                last.then_inc(kv_spread, 1)

            def scores(b):
                pe.wait_ge(evacuated, J_Q + b // 2 + 1)
                if b:
                    pe.wait_ge(logits_ready, b)
                if b == 0:
                    pe.wait_ge(scaled_keys, 1)
                    pe.wait_ge(kv_ready, 1)
                for t in range(TT):
                    nk = key_count(t)
                    for e in range(2):
                        last = nc.tensor.matmul(ps[:, e, P * t:P * t + nk], q_T[64 * e:64 * e + 64, b, t * P:(t + 1) * P],
                                                k_dup[64 * e:64 * e + 64, b // 4, 0:nk], start=True, stop=True)
                last.then_inc(scores_done, 1)

            def turn_probs(b):
                pe.wait_ge(probs_ready, b + 1)
                if b:
                    pe.wait_ge(att_ready, b)
                for e in range(2):
                    for m in range(2):
                        s = slice(256 + e * 256 + m * P, 256 + e * 256 + (m + 1) * P)
                        nc.tensor.transpose(ps[:, 2, e * 256 + m * P:e * 256 + (m + 1) * P], probs[b % 2][:, s], ident)
                for e in range(2):
                    last = nc.tensor.transpose(ps[:, 3, e * P:(e + 1) * P], probs[b % 2][:, e * P:(e + 1) * P], ident)
                last.then_inc(probs_turned, 1)

            def probs_values(b):
                pe.wait_ge(probs_T_ready, 2 * b + 2)
                kv = slice(64 * (b // 4), 64 * (b // 4) + 64)
                for e in range(2):
                    o = ps[64 * e:64 * e + 64, 3, 256:512]
                    nc.tensor.matmul(o[:, 0:P], v_att[:, 0, kv], probs_T[:, e * P:(e + 1) * P], start=True, stop=True)
                    for m in range(2):
                        s = slice(256 + e * 256 + m * P, 256 + e * 256 + (m + 1) * P)
                        last = nc.tensor.matmul(o[:, P:2 * P], v_att[:, m, kv], probs_T[:, s], start=(m == 0), stop=(m == 1))
                last.then_inc(pv_done, 1)

            def ret_qk(h):
                for m in range(2):
                    for e in range(2):
                        o = ps[:, h, 0:T] if m == 0 else ps[:, h, T:T + P]
                        last = nc.tensor.matmul(o, qk_ret[:, PAIRS + 2 * h + e, m * P:(m + 1) * P],
                                                qk_ret[:, 2 * h + e, m * P:T], start=(e == 0), stop=(e == 1))
                last.then_inc(qk_done, 1)

            def ret_values(h):
                v = slice(h * RET_HEAD, (h + 1) * RET_HEAD)
                nc.tensor.matmul(ps[:, h, 0:256], decay[:, h, 0:P], v_ret[:, 0, v], start=True, stop=True)
                nc.tensor.matmul(ps[:, h, 256:512], decay[:, h, P:2 * P], v_ret[:, 0, v], start=True, stop=False)
                nc.tensor.matmul(ps[:, h, 256:512], decay[:, h, 2 * P:3 * P], v_ret[:, 1, v], start=False, stop=True).then_inc(ret_done, 1)

            def turn_ret(h):
                pe.wait_ge(ret_normed, h + 1)
                for e in range(2):
                    for t in range(TT):
                        last = nc.tensor.transpose(ps[:, h, e * T + t * P:e * T + (t + 1) * P],
                                                   gate[:, t, (2 * h + e) * P:(2 * h + e + 1) * P], ident)
                last.then_inc(ret_turned, 1)

            def spread_gate(n, bank):
                nc.tensor.matmul(ps[:, bank, :], ones[:, :], acc[:, 0, n * 512:(n + 1) * 512], start=True, stop=True).then_inc(gate_spread, 1)

            for j in range(J_MLP):
                kind = JOBS[j][0]
                for q in range(N_GROUPS[j]):
                    g = FIRST[j] + q
                    pe.wait_ge(lo_ready, PRE + g + 1)
                    if q == 0 and j >= 2:
                        pe.wait_ge(evacuated, j - 1)
                    if j == 0:
                        pe.wait_ge(act_ready, 2 * (q + 1))
                    if j == J_OA and q == 0:
                        pe.wait_ge(att_ready, PAIRS)
                    if j == J_OR:
                        pe.wait_ge(ret_ready, 4 * q + 4)
                    if kind == "feat":
                        feature_group(8 * q, g % 2, j % 2, q == 1)
                    elif kind == "tok":
                        token_group(act_hl, 4 * q, g % 2, j % 2, q == 0, q == 3)
                    elif kind == "out_attn":
                        token_group(attn_hl, 4 * q, g % 2, j % 2, q == 0, q == 1)
                    else:
                        token_group(act_hl, PAIRS + 4 * q, g % 2, j % 2, q == 0, q == 1)
                    if j == 1 and q == 1:
                        spread_kv()
                    if pair_at(g, 6) is not None:
                        probs_values(pair_at(g, 6))
                    if pair_at(g, 5) is not None:
                        turn_probs(pair_at(g, 5))
                    if pair_at(g, 1) is not None:
                        scores(pair_at(g, 1))
                    if j == J_VR and q == 0:
                        pe.wait_ge(att_ready, PAIRS)
                        pe.wait_ge(ada_used, 2 * KT)
                        sum_mod(1, 3, 0)
                    if j == J_VR + 1 and q == 0:
                        pe.wait_ge(mod_ready, 3)
                        for h in range(RET_HEADS):
                            ret_qk(h)
                    if j == J_OA and q == 1:
                        pe.wait_ge(qk_decayed, RET_HEADS)
                        pe.wait_ge(evacuated, J_OA)
                        for h in range(RET_HEADS):
                            ret_values(h)
                    if g in (FIRST[J_OA] + 4, FIRST[J_OA] + 5):
                        turn_ret(2 * (g - FIRST[J_OA] - 4))
                        turn_ret(2 * (g - FIRST[J_OA] - 4) + 1)
                    if j >= J_OR - 1 and j < J_MLP - 1 and q == 1:
                        n = j + 1 - J_OR
                        if n == 0:
                            pe.wait_ge(ret_ready, 2 * RET_HEADS)
                            pe.wait_ge(ada_used, KT)
                        if n >= 2:
                            pe.wait_ge(gate_copied, n - 1)
                        spread_gate(n, n % 2)
                    if j == J_MLP - 1 and q == 0:
                        pe.wait_ge(ada_used, 3 * KT)
                        sum_mod(1, 3, 0)

            pe.wait_ge(mod_ready, 4)
            turn_normed(xn2, False)

            PB = J_MLP % 2

            def w1_two(g, j, first):
                for jj in range(2):
                    for q in range(2):
                        u = 2 * jj + q
                        pe.wait_ge(lo_ready, PRE + 1 + u + g)
                        if q == 0:
                            pe.wait_ge(evacuated, j - 1 + jj)
                        if first and jj == 0:
                            pe.wait_ge(act_ready, 4 + 2 * (q + 1))
                        feature_group(8 * q, u % 2, (PB + jj) % 2, q == 1)

            def w1_block(g0, j0, first):
                if first:
                    w1_two(g0, j0, True)
                    with pe.Fori(1, F_JOBS // 2) as m:
                        w1_two(g0 + m * 4, j0 + m * 2, False)
                else:
                    with pe.Fori(0, F_JOBS // 2) as m:
                        w1_two(g0 + m * 4, j0 + m * 2, False)

            def w2_block(g0, j0, blocks_done, last):
                for jj in range(STRIPS):
                    for q in range(T_GROUPS):
                        pe.wait_ge(lo_ready, PRE + 1 + 4 * jj + q + g0)
                        if q == 0:
                            pe.wait_ge(evacuated, j0 + jj - 1)
                        if jj == 0 and q == 0:
                            pe.wait_ge(hid_ready, blocks_done - 1)
                        if jj == 0 and q == T_GROUPS - 1:
                            pe.wait_ge(hid_ready, blocks_done)
                        token_group(hid_hl, 4 * q, q % 2, (PB + jj) % 2, q == 0, q == T_GROUPS - 1)
                        if last and q == 0:
                            if jj == 0:
                                pe.wait_ge(ada_used, 4 * KT)
                            if jj >= 2:
                                pe.wait_ge(gate_copied, STRIPS + jj - 1)
                            spread_gate(jj, jj % 2)

            w1_block(G_MLP, J_MLP, True)
            with pe.Fori(0, SUPER - 1) as s:
                w2_block(G_MLP + 16 + s * 32, J_MLP + 8 + s * 12, 8 + s * 8, False)
                w1_block(G_MLP + 32 + s * 32, J_MLP + 12 + s * 12, False)
            w2_block(G_MLP + 16 + 32 * (SUPER - 1), J_MLP + 8 + 12 * (SUPER - 1), 8 * SUPER, True)

        @block.vector
        def _(dve):
            steps = [0]

            def link(ins):
                steps[0] += 1
                ins.then_inc(vec_step, 1)
                dve.wait_ge(vec_step, steps[0])

            dve.wait_ge(vec_turned, 1)
            nc.vector.tensor_copy(vec_T, ps[:, 0, 0:64]).then_inc(vec_ready, 1)
            dve.wait_ge(vec_ready, 1)

            def sum_tile(n):
                a, k = n % 2, n // 2
                dve.wait_ge(stage_full[n % STAGES], 16 * (n // STAGES + 1))
                if k:
                    dve.wait_ge(lo_ready, n - 1)
                else:
                    dve.wait_ge(bias_loaded[a], 16)
                nc.vector.scalar_tensor_tensor(out=acc[:, a, :], in0=stage[:, n % STAGES, :], scalar=vec_T[:, V_C + k:V_C + k + 1],
                                               in1=acc[:, a, :], op0=ALU.mult, op1=ALU.add).then_inc(lo_ready, 1)

            def row_norm(total, roots):
                nc.vector.tensor_scalar(mean_sq, total, 1.0 / D, EPS, ALU.mult, ALU.add).then_inc(var_ready, 1)
                dve.wait_ge(std_ready, roots)
                link(nc.vector.reciprocal(rstd, std))
                return refine(rstd, mean_sq, newton[:, 0:2])

            def refine(r, v, step):
                link(nc.vector.tensor_tensor(step, r, r, ALU.mult))
                link(nc.vector.scalar_tensor_tensor(out=step, in0=step, scalar=-0.5, in1=v, op0=ALU.mult, op1=ALU.mult))
                return nc.vector.scalar_tensor_tensor(out=r, in0=step, scalar=1.5, in1=r, op0=ALU.add, op1=ALU.mult)

            for n in range(PRE):
                sum_tile(n)
                if n == 11:
                    dve.wait_ge(squares, 2)
                    link(row_norm(sq_sum[:, 0:2], 1))
                    for t in range(TT):
                        last = nc.vector.tensor_scalar(xn[:, t, :], x_sb[:, t, :], rstd[:, t:t + 1], None, ALU.mult)
                        if t == 0:
                            link(last)
                    last.then_inc(normed, 1)
                if n == 14:
                    dve.wait_ge(sinks_loaded, 16)
                    s4 = sink4.rearrange("p (b t e) -> p b t e", b=PAIRS, t=2)
                    n4 = nsink4.rearrange("p (b t e) -> p b t e", b=PAIRS, t=2)
                    for t in range(TT):
                        nc.vector.tensor_copy(s4[:, :, t, :], sink_row.rearrange("p (b e) -> p b e", e=2))
                        link(nc.vector.tensor_scalar(n4[:, :, t, :], sink_row.rearrange("p (b e) -> p b e", e=2), -1.0, None, ALU.mult))

            dve.wait_ge(mod_summed, 1)
            nc.vector.scalar_tensor_tensor(out=scale1, in0=ps[:, 0, 0:KT], scalar=1.0, in1=vec_T[:, V_MIX:V_MIX + KT],
                                           op0=ALU.add, op1=ALU.mult).then_inc(mod_ready, 1)
            dve.wait_ge(mod_summed, 2)
            nc.vector.tensor_copy(shift1, ps[:, 1, 0:KT]).then_inc(mod_ready, 1)
            dve.wait_ge(mod_ready, 2)
            dve.wait_ge(turned_out, 8)

            def modulate(q):
                for k in range(4 * q, 4 * q + 4):
                    nc.vector.tensor_scalar(xn_T[:, k, :], xn_T[:, k, :], scale1[:, k:k + 1], shift1[:, k:k + 1],
                                            ALU.mult, ALU.add).then_inc(h_ready, 1)

            def modulated_tail(source, q, hi):
                dve.wait_ge(mod_hi, hi)
                nc.vector.tensor_tensor(act_hl[:, 4 * q:4 * q + 4, T:2 * T], source[:, 4 * q:4 * q + 4, :],
                                        act_hl[:, 4 * q:4 * q + 4, 0:T].bitcast(F32), ALU.subtract).then_inc(act_ready, 1)

            def split_group(g, slot, ring, n_hi):
                dve.wait_ge(hi_ready, n_hi)
                if not isinstance(g, int) or g >= 2:
                    dve.wait_ge(group_used, g - 1)
                nc.vector.tensor_tensor(w_lo[:, ring, :], stage[:, slot, :], w_hi[:, ring, :].bitcast(F32), ALU.subtract).then_inc(lo_ready, 1)

            modulate(0)
            modulate(1)
            modulated_tail(xn_T, 0, 1)
            modulated_tail(xn_T, 1, 2)
            split_group(0, 0, 0, 1)
            modulate(2)
            modulate(3)
            modulated_tail(xn_T, 2, 3)
            modulated_tail(xn_T, 3, 4)
            split_group(1, 1, 1, 2)

            def sum_cross(dst, pair, crossed):
                dve.wait_ge(cross_copied, crossed)
                nc.vector.tensor_tensor(dst, ps_job[:, 2 * pair:2 * pair + 2, 0:T], tmp[:, :, :], ALU.add).then_inc(evacuated, 1)

            def logits(b):
                dve.wait_ge(scores_done, b + 1)
                for t in range(TT):
                    nk, at = key_count(t), 256 * t
                    for e in range(2):
                        h = 2 * b + e
                        slope = 2.0 ** (-8.0 * (h + 1) / (2 * PAIRS))
                        last = nc.vector.scalar_tensor_tensor(out=probs[b % 2][:, at + e * nk:at + (e + 1) * nk], in0=dist[:, P * t:P * t + nk],
                                                              scalar=float(np.float32(slope)), in1=ps[:, e, P * t:P * t + nk],
                                                              op0=ALU.mult, op1=ALU.add)
                        if (t, e) != (TT - 1, 1):
                            steps[0] += 1
                            last.then_inc(vec_step, 1)
                link(last)
                for t in range(TT):
                    nk, at = key_count(t), 256 * t
                    last = nc.vector.tensor_reduce(mx[:, 2 * t:2 * t + 2], probs[b % 2][:, at:at + 2 * nk].rearrange("p (e n) -> p e n", e=2), AX_X, ALU.max)
                    if t == 0:
                        steps[0] += 1
                        last.then_inc(vec_step, 1)
                link(last)
                link(nc.vector.scalar_tensor_tensor(out=nmax, in0=mx, scalar=-1.0, in1=nsink4[:, 4 * b:4 * b + 4], op0=ALU.mult, op1=ALU.min))
                nc.vector.tensor_tensor(d_sink, sink4[:, 4 * b:4 * b + 4], nmax, ALU.add).then_inc(logits_ready, 1)

            def normalise(b):
                dve.wait_ge(exp_done, 5 * b + 5)
                link(nc.vector.tensor_tensor(p_den, p_sum, p_sink, ALU.add))
                link(nc.vector.reciprocal(p_inv, p_den))
                for t in range(TT):
                    nk, at = key_count(t), 256 * t
                    for e in range(2):
                        i = 2 * t + e
                        s = slice(at + e * nk, at + (e + 1) * nk)
                        last = nc.vector.tensor_scalar(probs[b % 2][:, s], probs[b % 2][:, s], p_inv[:, i:i + 1], None, ALU.mult)
                        if i < 3:
                            steps[0] += 1
                            last.then_inc(vec_step, 1)
                last.then_inc(probs_ready, 1)

            def attention_tail(b):
                dve.wait_ge(att_hi, b + 1)
                nc.vector.scalar_tensor_tensor(out=attn_hl[:, b, T:2 * T], in0=ps[:, 3, 256:512], scalar=vec_T[:, V_BETA + b:V_BETA + b + 1],
                                               in1=attn_hl[:, b, 0:T].bitcast(F32), op0=ALU.mult, op1=ALU.subtract).then_inc(att_ready, 1)

            def silu_gate(n, pair, part):
                cols = gate[:, :, n * 512:(n + 1) * 512]
                if part == 0:
                    dve.wait_ge(gate_exp, n + 1)
                    link(nc.vector.tensor_scalar(cols, cols, 1.0, None, ALU.add))
                if part < 2:
                    link(nc.vector.reciprocal(cols[:, part, :], cols[:, part, :]))
                else:
                    nc.vector.tensor_tensor(cols, ps_job[:, 2 * pair:2 * pair + 2, :], cols, ALU.mult).then_inc(evacuated, 1)

            def group_stats():
                for h in range(RET_HEADS):
                    dve.wait_ge(ret_done, h + 1)
                    for t in range(TT):
                        i = 2 * h + t
                        steps[0] += 1
                        nc.vector.bn_stats(bn6[:, 6 * i:6 * i + 6], ps[:, h, t * 256:(t + 1) * 256]).then_inc(vec_step, 1)
                dve.wait_ge(vec_step, steps[0])
                for i in range(2 * RET_HEADS):
                    steps[0] += 1
                    nc.vector.bn_aggr(bn2[:, 2 * i:2 * i + 2], bn6[:, 6 * i:6 * i + 6]).then_inc(vec_step, 1)
                dve.wait_ge(vec_step, steps[0])
                nc.vector.tensor_scalar(gn_var, bn2.rearrange("p (i m) -> p i m", m=2)[:, :, 1], EPS, None, ALU.add).then_inc(var_ready, 1)

            def group_norm(h):
                if h == 0:
                    dve.wait_ge(std_ready, 2)
                    link(nc.vector.reciprocal(gn_rstd, gn_std))
                    link(refine(gn_rstd, gn_var, newton))
                for t in range(TT):
                    i = 2 * h + t
                    s = gate[:, t, h * RET_HEAD:(h + 1) * RET_HEAD]
                    steps[0] += 1
                    nc.vector.scalar_tensor_tensor(out=s, in0=ps[:, h, t * 256:(t + 1) * 256], scalar=bn2[:, 2 * i:2 * i + 1],
                                                   in1=s, op0=ALU.subtract, op1=ALU.mult).then_inc(vec_step, 1)
                dve.wait_ge(vec_step, steps[0])
                for t in range(TT):
                    i = 2 * h + t
                    s = gate[:, t, h * RET_HEAD:(h + 1) * RET_HEAD]
                    last = nc.vector.tensor_scalar(s, s, gn_rstd[:, i:i + 1], None, ALU.mult)
                    if t == 0:
                        steps[0] += 1
                        last.then_inc(vec_step, 1)
                last.then_inc(ret_normed, 1)

            def retention_tail(h):
                dve.wait_ge(ret_hi, 2 * h + 2)
                for e in range(2):
                    k = 2 * h + e
                    nc.vector.scalar_tensor_tensor(out=act_hl[:, PAIRS + k, T:2 * T], in0=ps[:, h, e * T:(e + 1) * T],
                                                   scalar=vec_T[:, V_GRET + k:V_GRET + k + 1], in1=act_hl[:, PAIRS + k, 0:T].bitcast(F32),
                                                   op0=ALU.mult, op1=ALU.subtract).then_inc(ret_ready, 1)

            def gated_strip(part, n, spread):
                s = slice(n * 512, (n + 1) * 512)
                dve.wait_ge(gate_copied, spread)
                gate_n = tmp.rearrange("p a n -> p (a n)")
                dve.wait_ge(x_reloaded, 16)
                steps[0] += 1
                for t in range(TT):
                    last = nc.vector.tensor_tensor(part[:, t, s], part[:, t, s], gate_n, ALU.mult)
                    if t == 0:
                        last.then_inc(vec_step, 1)
                link(last)
                link(nc.vector.tensor_tensor(x_sb[:, :, s], x_sb[:, :, s], part[:, :, s], ALU.add))

            def add_residual(part, n, j, pair, used):
                s = slice(n * 512, (n + 1) * 512)
                gate_n = tmp.rearrange("p a n -> p (a n)")
                dve.wait_ge(group_used, used)
                steps[0] += 1
                nc.vector.tensor_tensor(part[:, 0, s], ps_job[:, 2 * pair, :], gate_n, ALU.mult).then_inc(vec_step, 1)
                nc.vector.tensor_tensor(part[:, 1, s], ps_job[:, 2 * pair + 1, :], gate_n, ALU.mult).then_inc(evacuated, 1)
                dve.wait_ge(vec_step, steps[0])
                dve.wait_ge(evacuated, j + 1)
                nc.vector.tensor_tensor(x_sb[:, :, s], x_sb[:, :, s], part[:, :, s], ALU.add).then_inc(x_updated, 1)

            def take_out(j):
                pair, used = j % 2, FIRST[j + 1]
                kind = JOBS[j][0]
                if kind == "feat":
                    if j == 0:
                        dst = tmp[:, :, :]
                    elif j < J_QKR:
                        dst = q_T[:, 2 * (j - J_Q):2 * (j - J_Q) + 2, :]
                    else:
                        dst = qk_ret[:, 2 * (j - J_QKR):2 * (j - J_QKR) + 2, :]
                    sum_cross(dst, pair, j + 1)
                elif kind == "tok":
                    n = j - J_VR
                    dve.wait_ge(group_used, used)
                    nc.vector.tensor_copy(v_ret[:, :, n * 512:(n + 1) * 512], ps_job[:, 2 * pair:2 * pair + 2, :]).then_inc(evacuated, 1)
                elif kind == "out_attn":
                    n = j - J_OA
                    dve.wait_ge(group_used, used)
                    nc.vector.tensor_copy(y_part[:, :, n * 512:(n + 1) * 512], ps_job[:, 2 * pair:2 * pair + 2, :]).then_inc(evacuated, 1)
                else:
                    n = j - J_OR
                    add_residual(y_part, n, j, pair, used)

            for j in range(J_MLP):
                for q in range(N_GROUPS[j]):
                    g = FIRST[j] + q
                    if g >= 2:
                        split_group(g, g % STAGES, g % 2, g + 1)
                    if pair_at(g, 8) is not None:
                        attention_tail(pair_at(g, 8))
                    if pair_at(g, 4) is not None:
                        normalise(pair_at(g, 4))
                    if j >= 1:
                        if J_GR <= j - 1 < J_VR:
                            if q >= 1:
                                silu_gate(j - 1 - J_GR, (j - 1) % 2, q - 1)
                        elif q == (0 if j - 1 >= J_OR else 1):
                            take_out(j - 1)
                    if j == 2 and q == 1:
                        dve.wait_ge(kv_spread, 2)
                        nc.vector.tensor_copy(v_att[:, :, :], ps[:, 1, 0:256].rearrange("p (t n) -> p t n", t=2)).then_inc(kv_ready, 1)
                    if pair_at(g, 3) is not None:
                        logits(pair_at(g, 3))
                    if j == J_VR and q == 2:
                        dve.wait_ge(mod_summed, 3)
                        nc.vector.tensor_copy(shift2, ps[:, 3, 0:KT]).then_inc(mod_ready, 1)
                    if j == J_VR + 1 and q == 2:
                        dve.wait_ge(decay_loaded, 16)
                        for h in range(RET_HEADS):
                            dve.wait_ge(qk_done, h + 1)
                            nc.vector.tensor_tensor(decay[:, h, :], ps[:, h, 0:384], decay[:, h, :], ALU.mult).then_inc(qk_decayed, 1)
                    if g == FIRST[J_OA] + 3:
                        group_stats()
                    if g in (FIRST[J_OA] + 4, FIRST[J_OA] + 5):
                        group_norm(2 * (g - FIRST[J_OA] - 4))
                        group_norm(2 * (g - FIRST[J_OA] - 4) + 1)
                    if g in (FIRST[J_OA] + 6, FIRST[J_OA] + 7):
                        retention_tail(2 * (g - FIRST[J_OA] - 6))
                        retention_tail(2 * (g - FIRST[J_OA] - 6) + 1)
                    if j >= J_OR and q == 1:
                        gated_strip(y_part, j - J_OR, j - J_OR + 1)
            split_group(G_MLP, G_MLP % STAGES, 0, G_MLP + 1)
            take_out(J_MLP - 1)

            dve.wait_ge(mod_summed, 4)
            nc.vector.scalar_tensor_tensor(out=scale2, in0=ps[:, 3, 0:KT], scalar=1.0, in1=vec_T[:, V_FFN:V_FFN + KT],
                                           op0=ALU.add, op1=ALU.mult).then_inc(mod_ready, 1)
            dve.wait_ge(squares, 2 + 2 * STRIPS)
            link(nc.vector.tensor_reduce(bn2[:, 0:2], sq_sum.rearrange("p (t n) -> p t n", t=TT), AX_X, ALU.add))
            link(row_norm(bn2[:, 0:2], 3))
            for n in range(STRIPS):
                cols = slice(n * TOK_COLS, (n + 1) * TOK_COLS)
                nc.vector.tensor_scalar(xn2[:, 0, cols], x_sb[:, 0, cols], rstd[:, 0:1], None, ALU.mult)
                nc.vector.tensor_scalar(xn2[:, 1, cols], x_sb[:, 1, cols], rstd[:, 1:2], None, ALU.mult).then_inc(normed, 1)
            split_group(G_MLP + 1, (G_MLP + 1) % STAGES, 1, G_MLP + 2)
            dve.wait_ge(group_used, G_MLP)
            for q in range(4):
                dve.wait_ge(h_ready, KT + 4 * q + 4)
                nc.vector.tensor_copy(act_hl[:, 4 * q:4 * q + 4, 0:T], h2_T[:, 4 * q:4 * q + 4, :]).then_inc(mod_hi, 1)
                modulated_tail(h2_T, q, 4 + q + 1)

            PB = J_MLP % 2

            def hidden(n, crossed, j_done, pair):
                sum_cross(tmp[:, :, :], pair, crossed)
                dve.wait_ge(evacuated, j_done)
                nc.vector.scalar_tensor_tensor(out=tmp[:, :, :], in0=tmp[:, :, :], scalar=0.0, in1=tmp[:, :, :],
                                               op0=ALU.max, op1=ALU.mult).then_inc(hid_f32, 1)

            def hidden_tail(n, k0):
                dve.wait_ge(hid_hi, n + 1)
                nc.vector.tensor_tensor(hid_hl[:, bass.ds(k0, 2), T:2 * T], tmp[:, :, :], hid_hl[:, bass.ds(k0, 2), 0:T].bitcast(F32),
                                        ALU.subtract).then_inc(hid_ready, 1)

            N_FEAT = J_GR

            def add_strip(jj, used, pair):
                s = slice(jj * 512, (jj + 1) * 512)
                dve.wait_ge(group_used, used)
                dve.wait_ge(f_zeroed, 1)
                nc.vector.tensor_tensor(f_acc[:, :, s], f_acc[:, :, s], ps_job[:, 2 * pair:2 * pair + 2, :], ALU.add).then_inc(evacuated, 1)

            def w1_rest(n0, g0, j0):
                with dve.Fori(0, F_JOBS // 2 - 1) as m:
                    for jj in range(2):
                        for q in range(2):
                            u = 2 * jj + q
                            g = g0 + 4 + u + m * 4
                            split_group(g, (G_MLP + u) % STAGES, u % 2, g + 1)
                            n = n0 + 1 + jj + m * 2
                            if q == 0:
                                hidden(n, N_FEAT + 1 + n, j0 + 2 + jj + m * 2, (PB + 1 + jj) % 2)
                            else:
                                hidden_tail(n, m * 4 + 2 + 2 * jj)

            def w1_first(n0, g0, j0, after_w2):
                for u in range(4):
                    if u >= 2 or after_w2:
                        split_group(g0 + u, (G_MLP + u) % STAGES, u % 2, g0 + u + 1)
                    if u == 0 and after_w2:
                        add_strip(STRIPS - 1, g0, (PB + 1) % 2)
                    if u == 2:
                        hidden(n0, N_FEAT + 1 + n0, j0 + 1, PB)
                    if u == 3:
                        hidden_tail(n0, 0)

            def w2_block(g0, j0, n_last, last):
                for jj in range(STRIPS):
                    for q in range(T_GROUPS):
                        u = 4 * jj + q
                        split_group(g0 + u, (G_MLP + u) % STAGES, u % 2, g0 + u + 1)
                        if jj == 0 and q == 0:
                            hidden(n_last, N_FEAT + 1 + n_last, j0, (PB + 1) % 2)
                        if jj == 0 and q == 1:
                            hidden_tail(n_last, KT - 2)
                        if jj > 0 and q == 0:
                            if last:
                                add_residual(f_acc, jj - 1, j0 + jj - 1, (PB + jj - 1) % 2, g0 + 4 * jj)
                            else:
                                add_strip(jj - 1, g0 + 4 * jj, (PB + jj - 1) % 2)
                        if last and q == 3:
                            gated_strip(f_acc, jj, STRIPS + jj + 1)

            w1_first(0, G_MLP, J_MLP, False)
            w1_rest(0, G_MLP, J_MLP)
            with dve.Fori(0, SUPER - 1) as s:
                w2_block(G_MLP + 16 + s * 32, J_MLP + 8 + s * 12, 7 + s * 8, False)
                w1_first(8 + s * 8, G_MLP + 32 + s * 32, J_MLP + 12 + s * 12, True)
                w1_rest(8 + s * 8, G_MLP + 32 + s * 32, J_MLP + 12 + s * 12)
            gl, jl = G_MLP + 16 + 32 * (SUPER - 1), J_MLP + 8 + 12 * (SUPER - 1)
            w2_block(gl, jl, 8 * SUPER - 1, True)
            add_residual(f_acc, STRIPS - 1, jl + 3, (PB + 3) % 2, gl + 16)

            dve.wait_ge(squares, 2 + 4 * STRIPS)
            link(nc.vector.tensor_reduce(bn2[:, 0:2], sq_sum.rearrange("p (t n) -> p t n", t=TT), AX_X, ALU.add))
            row_norm(bn2[:, 0:2], 4).then_inc(normed, 1)
            dve.wait_ge(normed, 2 + STRIPS)
            dve.wait_ge(gfin_loaded, 16)
            for t, n in VEC_PIECES:
                cols = slice(n * TOK_COLS, (n + 1) * TOK_COLS)
                nc.vector.scalar_tensor_tensor(out=x_sb[:, t, cols], in0=x_sb[:, t, cols], scalar=rstd[:, t:t + 1],
                                               in1=acc[:, 1, cols], op0=ALU.mult, op1=ALU.mult).then_inc(out_ready, 1)


_INS = ["x", "c", "w_ada", "b_ada", "g_mix", "w_in", "beta_attn", "sinks", "g_ret", "w_out", "g_ffn", "w1", "w2", "g_final"]


def shape_constants():
    tok = np.arange(T)
    consts = np.zeros((P, P + 384), np.float32)
    consts[:, 0:P] = np.eye(P)
    for t in range(TT):
        q = tok[t * P:(t + 1) * P, None]
        k = tok[None, 0:P * (t + 1)]
        behind = q // CHUNK - k // CHUNK
        keep = (behind >= 0) & (behind <= 1)
        consts[:, P + P * t:P + P * t + P * (t + 1)] = np.where(keep, -np.abs(q - k), -1e34)
    log_g = np.log(1.0 - 2.0 ** (-5.0 - np.arange(RET_HEADS, dtype=np.float64)))
    decay = np.zeros((RET_HEADS, P, 384), np.float32)
    k, q = tok[:, None], tok[None, :]
    for h in range(RET_HEADS):
        full = np.where(k // CHUNK <= q // CHUNK, np.exp(log_g[h] * np.abs(q - k)), 0.0) * RET_HEAD ** -0.5
        decay[h, :, 0:T] = full[0:P]
        decay[h, :, T:384] = full[P:T, P:T]
    return consts, decay


def kernel(**inputs):
    import concourse.bacc as _bacc
    from concourse.bass_utils import run_bass_kernel_spmd as _run

    nc = _bacc.Bacc("TRN2", target_bir_lowering=False, num_devices=1)
    arrays = {f"in_{n}": np.ascontiguousarray(inputs[n]) for n in _INS}
    arrays["in_consts"], arrays["in_decay"] = shape_constants()
    args = [nc.dram_tensor(n, a.shape, mybir.dt.from_np(a.dtype), kind="ExternalInput").ap() for n, a in arrays.items()]
    out = nc.dram_tensor("out_y", (1, T, D), F32, kind="ExternalOutput").ap()
    build(nc, *args, out)
    r = _run(nc, [arrays], core_ids=[0])
    return r.results[0]["out_y"]
```

```python
from contextlib import ExitStack

import numpy as np

import concourse.bass as bass
from concourse import mybir

F32 = mybir.dt.float32
F32R = mybir.dt.float32r
ACT = mybir.ActivationFunctionType
ALU = mybir.AluOpType
AX_X = mybir.AxisListType.X

P = 128
D = 2048
T = 256
TT = T // P
KT = D // P
CHUNK = 64
HEAD = 64
KV_COLS = 128
ATTN = D // 2
RET_HEAD = 256
RET_HEADS = (D - ATTN) // RET_HEAD
PAIRS = ATTN // P
FF = 4 * D
EPS = 1e-6
G = 2048
STAGES = 4
FEAT_COLS = 256
TOK_COLS = 512
STRIPS = D // TOK_COLS

Q0 = 0
KV0 = ATTN
QR0 = ATTN + 2 * KV_COLS
KR0 = QR0 + D - ATTN
VR0 = KR0 + D - ATTN
GR0 = VR0 + D - ATTN

HALF = KT // 2


def w_in_jobs(k0, between):
    jobs = [("feat", KV0, k0, HALF)]
    jobs += [("feat", Q0 + FEAT_COLS * n, k0, HALF) for n in range(4)] + between
    jobs += [("feat", QR0 + FEAT_COLS * n, k0, HALF) for n in range(8)]
    jobs += [("tok", GR0 + TOK_COLS * n, k0, HALF) for n in range(2)]
    return jobs + [("tok", VR0, k0, HALF)]


JOBS = w_in_jobs(0, []) + w_in_jobs(HALF, [("tok", VR0 + TOK_COLS, 0, KT)])
JOBS += [("out_attn", TOK_COLS * n, 0, HALF) for n in range(STRIPS)]
JOBS += [("out_ret", TOK_COLS * n, HALF, HALF) for n in range(STRIPS)]
J_B = len(w_in_jobs(0, []))
J_BQ, J_BGR = J_B + 1, J_B + 14
J_OA = J_BGR + 3
J_OR = J_OA + STRIPS
J_MLP = J_OR + STRIPS
N_GROUPS = [nk // (8 if kind == "feat" else 4) for kind, _, _, nk in JOBS]
FIRST = [sum(N_GROUPS[:j]) for j in range(len(JOBS) + 1)]
LAST_GROUP = [f - 1 for f in FIRST[1:]]
G_B, G_OA = FIRST[J_B], FIRST[J_OA]
SH2_PAIR = 5
SILU_AT = [G_OA - 2, G_OA - 1, G_OA, G_OA + 1, G_OA + 2, G_OA + 5]
SUPER = FF // D
G_MLP = FIRST[J_MLP]
F_JOBS = D // FEAT_COLS
T_GROUPS = 4

SH1, SC1, GT1, SH2, SC2, GT2 = (n * D for n in range(6))
POOL_UNITS = [(SH2, 0), (GT1, 1), (SC2, 0), (GT2, 1)]
PRE = 2 * KT

ITEMS = [("tile", n) for n in range(KT)]
for _g in range(FIRST[J_MLP]):
    while sum(i[0] == "tile" for i in ITEMS) < KT + min(KT, (7 * _g + 6) // 8):
        ITEMS.append(("tile", sum(i[0] == "tile" for i in ITEMS)))
    ITEMS.append(("group", _g))
ITEM_OF_GROUP = [i for i, item in enumerate(ITEMS) if item[0] == "group"]
ITEM_OF_TILE = [i for i, item in enumerate(ITEMS) if item[0] == "tile"]

ADA_4, ADA_3 = 35, 47
ADA_AHEAD = 3
ADA_START = 16
ADA_BEFORE_MLP = 3 * KT

VEC_PIECES = [(0, 0), (0, 1), (0, 2), (0, 3), (1, 0), (1, 1)]
POOL_PIECES = [(1, 2), (1, 3)]

V_MIX, V_FFN, V_BETA, V_GRET, V_C = 0, 16, 32, 40, 48


def key_count(t):
    return P * (t + 1)


def build(nc, x, c, w_ada, b_ada, g_mix, w_in, beta_attn, sinks, g_ret, w_out, g_ffn, w1, w2,
          g_final, consts, decay_in, out):
    with ExitStack() as ctx:
        base = 16512
        place = {"at": base}

        def region(kib):
            at = place["at"]
            place["at"] += int(kib * 1024)
            return at

        def sb(name, shape, dt, offset):
            return nc.alloc_sbuf_tensor_at(name, shape, dt, offset=offset)

        def sem(name):
            return ctx.enter_context(nc.semaphore(name))

        x_sb = sb("x_sb", [P, TT, D], F32, region(16))
        act_hl = sb("act_hl", [P, KT, 2 * T], F32R, region(32))
        y_at = region(32)
        xn_T = sb("xn_T", [P, KT, T], F32, y_at)
        gate = sb("gate", [P, TT, D - ATTN], F32, y_at)
        ada_y = sb("ada_y", [P, D], F32, y_at + 8192)
        qk_ret = sb("qk_ret", [P, 2 * PAIRS, T], F32, y_at + 16384)
        y_part = sb("y_part", [P, TT, D], F32, y_at + 16384)
        h2_T = sb("h2_T", [P, KT, T], F32, y_at)
        hid_hl = sb("hid_hl", [P, KT, 2 * T], F32R, y_at)
        stage = sb("stage", [P, STAGES, G], F32, region(32))
        w_hi = sb("w_hi", [P, 2, G], F32R, region(16))
        w_lo = sb("w_lo", [P, 2, G], F32R, region(16))
        acc = sb("acc", [P, 2, D], F32, region(16))
        ada = sb("ada", [P, 2, D], F32, region(16))
        r_at = region(16)
        q_T = sb("q_T", [P, PAIRS, T], F32, r_at)
        v_ret = sb("v_ret", [P, 2, TT, TOK_COLS], F32, r_at + 8192)
        f_acc = sb("f_acc", [P, TT, D], F32, r_at)
        k_dup = sb("k_dup", [P, 2, T], F32, region(2))
        v_att = sb("v_att", [P, TT, KV_COLS], F32, region(1))
        p_at = region(6)
        tmp_at = region(3)
        probs = [sb("probs_even", [P, 768], F32, p_at), sb("probs_odd", [P, 768], F32, tmp_at)]
        probs_T = sb("probs_T", [P, 768], F32, p_at + 3072)
        diag = sb("diag", [P, TT, P], F32, p_at)
        decay = sb("decay", [P, RET_HEADS, 384], F32, p_at)
        tmp = sb("tmp", [P, 2, T], F32, tmp_at)
        vec_rows = sb("vec_rows", [64, P], F32, tmp_at)
        gate_sig = sb("gate_sig", [P, TT, D - ATTN], F32, r_at)
        cst = sb("cst", [P, P + 384], F32, region(2))
        ident, dist = cst[:, 0:P], cst[:, P:P + 384]
        ones = sb("ones", [P, P], F32, region(0.5))
        small = sb("small", [P, 348], F32, region(348 / 256))
        assert place["at"] <= 229368
        vec_T = small[:, 0:64]
        scale1, shift1, scale2, shift2 = (small[:, 64 + 16 * n:80 + 16 * n] for n in range(4))
        sink4 = small[:, 128:160]
        nsink4 = small[:, 160:192]
        sink_row = small[:, 192:208]
        sq_sum = small[:, 208:216]
        rstd = small[:, 216:218]
        mean_sq = small[:, 218:220]
        mx = small[:, 220:224]
        nmax = small[:, 224:228]
        p_sum = small[:, 228:232]
        p_sink = small[:, 232:236]
        p_den = small[:, 236:240]
        p_inv = small[:, 240:244]
        bn6 = small[:, 244:292]
        bn2 = small[:, 292:308]
        gn_rstd = small[:, 308:316]
        d_sink = small[:, 316:320]
        gn_var, gn_std = small[:, 320:328], small[:, 328:336]
        std = small[:, 336:338]
        newton = small[:, 338:346]

        ps_job = ctx.enter_context(nc.psum_tensor("ps_job", [P, 4, 512], F32))
        ps = ctx.enter_context(nc.psum_tensor("ps", [P, 4, 512], F32))

        vec_loaded, x_loaded, cst_loaded, sinks_loaded = map(sem, ("vec_loaded", "x_loaded", "cst_loaded", "sinks_loaded"))
        decay_loaded, gfin_loaded, out_stored = map(sem, ("decay_loaded", "gfin_loaded", "out_stored"))
        bias_loaded = [sem(f"bias_loaded{n}") for n in range(2)]
        stage_full = [sem(f"stage_full{n}") for n in range(STAGES)]
        ada_full = [sem(f"ada_full{n}") for n in range(4)]
        hi_ready = sem("hi_ready")
        lo_ready = sem("lo_ready")
        group_used = sem("group_used")
        evacuated = sem("evacuated")
        cross_copied = sem("cross_copied")
        acc_zeroed, ada_scaled, ada_used, ones_set, act_scaled = map(
            sem, ("acc_zeroed", "ada_scaled", "ada_used", "ones_set", "act_scaled"))
        vec_turned, vec_ready, mod_summed, mod_ready = map(sem, ("vec_turned", "vec_ready", "mod_summed", "mod_ready"))
        squares, normed, turned, turned_out = map(sem, ("squares", "normed", "turned", "turned_out"))
        h_ready, mod_hi, act_ready = map(sem, ("h_ready", "mod_hi", "act_ready"))
        kv_spread, kv_ready, scaled_keys = map(sem, ("kv_spread", "kv_ready", "scaled_keys"))
        scores_done, logits_ready, exp_done, probs_ready = map(sem, ("scores_done", "logits_ready", "exp_done", "probs_ready"))
        probs_turned, probs_T_ready, pv_done, att_hi, att_ready = map(
            sem, ("probs_turned", "probs_T_ready", "pv_done", "att_hi", "att_ready"))
        qk_done, qk_decayed, gate_exp, ret_done, ret_normed = map(
            sem, ("qk_done", "qk_decayed", "gate_exp", "ret_done", "ret_normed"))
        ret_turned, ret_hi, ret_ready = map(sem, ("ret_turned", "ret_hi", "ret_ready"))
        gate_spread, gate_copied, x_updated, hid_f32, hid_hi, hid_ready, pool_out = map(
            sem, ("gate_spread", "gate_copied", "x_updated", "hid_f32", "hid_hi", "hid_ready", "pool_out"))
        vec_step = sem("vec_step")
        out_ready = sem("out_ready")
        x_reloaded = sem("x_reloaded")
        f_zeroed = sem("f_zeroed")
        var_ready, std_ready = map(sem, ("var_ready", "std_ready"))

        w_ada_v = w_ada[0].rearrange("(k p) n -> p k n", p=P)
        w_in_v = w_in[0].rearrange("(k p) n -> p k n", p=P)
        w_out_v = w_out[0].rearrange("(k p) n -> p k n", p=P)
        w1_v = w1[0].rearrange("(k p) n -> p k n", p=P)
        w2_v = w2[0].rearrange("(k p) n -> p k n", p=P)
        x_v = x[0].rearrange("(t p) n -> p t n", p=P)
        out_v = out[0].rearrange("(t p) n -> p t n", p=P)

        def group_source(j, q):
            kind, c0, k0, _ = JOBS[j]
            if kind == "feat":
                return w_in_v[:, k0:k0 + 8, c0:c0 + FEAT_COLS]
            w = w_in_v if kind == "tok" else w_out_v
            return w[:, k0 + 4 * q:k0 + 4 * q + 4, c0:c0 + TOK_COLS]

        def banks(j):
            if j >= J_MLP:
                return [2 * (j % 2), 2 * (j % 2) + 1]
            return [2 * (j % 2) + (j // 2) % 2] if JOBS[j][0] == "feat" else [2 * (j % 2), 2 * (j % 2) + 1]

        def jobs_out_before(j):
            return max([i + 1 for i in range(j) if set(banks(i)) & set(banks(j))], default=0)

        def psum_of(j):
            b = banks(j)
            return ps_job[:, b[0], :].rearrange("p (k n) -> p k n", k=2) if len(b) == 1 else ps_job[:, b[0]:b[1] + 1, :]

        def result_of(j):
            kind, c0, _, _ = JOBS[j]
            if c0 == KV0:
                return k_dup[:, :, :]
            if c0 < KV0:
                return q_T[:, c0 // P:c0 // P + 2, :]
            if kind == "feat":
                return qk_ret[:, (c0 - QR0) // P:(c0 - QR0) // P + 2, :]
            if c0 < GR0:
                return v_ret[:, (c0 - VR0) // TOK_COLS, :, :]
            return gate[:, :, c0 - GR0:c0 - GR0 + TOK_COLS]

        def ada_before(g):
            if g < ADA_START + 4:
                return min(ADA_AHEAD, g // 4)
            return min(ADA_BEFORE_MLP, ADA_AHEAD + (g - ADA_START - 4) * 4 // 3)

        def pair_at(g, step):
            b, odd = divmod(g - step - FIRST[J_BQ] - 1, 2)
            return b if not odd and 0 <= b < PAIRS else None

        ada_slots = [ada[:, 0, :], ada[:, 1, :], ada_y[:, :], x_sb[:, 1, :]]

        def ada_slot(n):
            if n < ADA_4:
                return (0, 1, 3)[n] if n < ADA_AHEAD else (0, 1, 3, 2)[(n - ADA_AHEAD) % 4]
            return (n - ADA_4) % 3 if n < ADA_3 else (n - ADA_3) % 2

        def ada_fill(n):
            return sum(ada_slot(i) == ada_slot(n) for i in range(n + 1))

        def ada_prev(m):
            return max([i for i in range(m) if ada_slot(i) == ada_slot(m)], default=-1)

        ada_loads = [[] for _ in range(G_MLP)]
        at = 0
        for m in range(ADA_BEFORE_MLP):
            behind = 2 if m < ADA_4 else 1
            if m < ADA_AHEAD:
                at = 2
            elif m <= 2 * ADA_AHEAD:
                at = ADA_START + 1 + m - ADA_AHEAD + m // (2 * ADA_AHEAD) * 2
            else:
                at = max(at, next(g for g in range(4, G_MLP) if ada_before(g - 4) >= ada_prev(m) + behind or g == G_MLP - 1))
            ada_loads[at].append(m)

        block = ctx.enter_context(nc.Block())

        @block.sync
        def _(sp):
            def load_group(src, slot, read):
                if not isinstance(read, int) or read > 0:
                    sp.wait_ge(lo_ready, read)
                sp.dma_start(stage[:, slot, :].rearrange("p (k n) -> p k n", k=src.shape[1]), src).then_inc(stage_full[slot], 16)

            def ada_source(m):
                return w_ada[0, (m % KT) * P:(m % KT + 1) * P, POOL_UNITS[m // KT][0]:POOL_UNITS[m // KT][0] + D]

            def load_tile(m):
                if ada_prev(m) >= 0:
                    sp.wait_ge(ada_used, ada_prev(m) + 1)
                sp.dma_start(ada_slots[ada_slot(m)], ada_source(m)).then_inc(ada_full[ada_slot(m)], 16)

            sources = [group_source(j, q) for j in range(J_MLP) for q in range(N_GROUPS[j])]
            for i, (what, n) in enumerate(ITEMS):
                if what == "tile":
                    k, c0 = n % KT, n // KT * (D // 2)
                    src = w_ada[0, k * P:(k + 1) * P, :].rearrange("p (v n) -> p v n", v=6)[:, 0:2, c0:c0 + D // 2]
                else:
                    src = sources[n]
                    for m in ada_loads[n]:
                        if m == 2:
                            sp.wait_ge(turned, 8)
                        if m == 2 * ADA_AHEAD:
                            sp.wait_ge(act_ready, 4)
                        load_tile(m)
                        if m == ADA_4 + 2:
                            sp.wait_ge(ada_used, ADA_4)
                            sp.dma_start(x_sb[:, 1, :], x_v[:, 1, :]).then_inc(x_reloaded, 16)
                load_group(src, i % STAGES, i - STAGES + 1)
                if (what, n) == ("group", G_OA + 3):
                    sp.wait_ge(pv_done, PAIRS)
                    sp.dma_start(decay[:, :, :], decay_in.rearrange("h p n -> p h n")).then_inc(decay_loaded, 16)

            def w1_groups(row, g0):
                for u in range(4):
                    src = w1_v[:, 8 * (u % 2):8 * (u % 2) + 8, bass.ds(row + FEAT_COLS * (u // 2), FEAT_COLS)]
                    g = g0 + u
                    load_group(src, (G_MLP + u) % STAGES, PRE + g - STAGES + 1)

            def w1_block(s, g0, m0=0):
                with sp.Fori(m0, F_JOBS // 2) as m:
                    w1_groups(s * D + m * (2 * FEAT_COLS), g0 + m * 4)

            def w2_block(s, g0, with_ada):
                def job(n, n_static):
                    if with_ada:
                        m = ADA_BEFORE_MLP + 4 + n_static
                        sp.wait_ge(ada_used, s * 4 + (m - 1))
                        rows = w_ada_v[:, bass.ds(s * 4 + (m % KT), 1), GT2:GT2 + D].rearrange("p a n -> p (a n)")
                        sp.dma_start(ada_slots[ada_slot(m)], rows).then_inc(ada_full[ada_slot(m)], 16)
                    for q in range(T_GROUPS):
                        src = w2_v[:, bass.ds(s * KT + 4 * q, 4), bass.ds(n * TOK_COLS, TOK_COLS)]
                        g = g0 + n * T_GROUPS + q
                        load_group(src, (G_MLP + q) % STAGES, PRE + g - STAGES + 1)

                if with_ada:
                    for n in range(STRIPS):
                        job(n, n)
                else:
                    with sp.Fori(0, STRIPS) as n:
                        job(n, None)

            load_tile(ADA_BEFORE_MLP)
            load_tile(ADA_BEFORE_MLP + 1)
            w1_groups(0, G_MLP)
            w1_groups(2 * FEAT_COLS, G_MLP + 4)
            load_tile(ADA_BEFORE_MLP + 2)
            load_tile(ADA_BEFORE_MLP + 3)
            w1_block(0, G_MLP, 2)
            with sp.Fori(0, SUPER - 1) as s:
                w2_block(s, G_MLP + 16 + s * 32, True)
                w1_block(s + 1, G_MLP + 32 + s * 32)
            w2_block(SUPER - 1, G_MLP + 16 + (SUPER - 1) * 32, False)
            sp.wait_ge(mod_ready, 4)
            sp.dma_start(acc[:, 0, :], g_final.rearrange("(a n) -> a n", a=1).to_broadcast([P, D])).then_inc(gfin_loaded, 16)

            def store(t, n):
                sp.dma_start(out_v[:, t, n * TOK_COLS:(n + 1) * TOK_COLS], x_sb[:, t, n * TOK_COLS:(n + 1) * TOK_COLS]).then_inc(out_stored, 16)

            for i, (t, n) in enumerate(VEC_PIECES):
                sp.wait_ge(out_ready, i + 1)
                store(t, n)
                if i % 3 == 2:
                    sp.wait_ge(pool_out, i // 3 + 1)
                    store(*POOL_PIECES[i // 3])
            sp.wait_ge(out_stored, 16 * TT * STRIPS)

        @block.gpsimd
        def _(pool):
            zeroed, biased = 0, [0, 0]

            def load_bias(dst, col, a):
                pool.dma_start(dst, b_ada[0:1, col:col + dst.shape[1]]).then_inc(bias_loaded[a], 16)
                biased[a] += 1

            def zero(a):
                nonlocal zeroed
                nc.gpsimd.memset(acc[:, a, :], 0.0).then_inc(acc_zeroed, 1)
                zeroed += 1
                pool.wait_ge(acc_zeroed, zeroed)

            for a in range(2):
                zero(a)
                load_bias(acc[0:1, a, 0:D // 2], SH1 + a * (D // 2), a)
                load_bias(acc[0:1, a, D // 2:D], SC1 + a * (D // 2), a)
            nc.gpsimd.memset(ones[:, :], 1.0).then_inc(ones_set, 1)

            def start_sum(u):
                col, a = POOL_UNITS[u]
                if col == GT2:
                    pool.wait_ge(gate_spread, STRIPS)
                else:
                    pool.wait_ge(mod_summed, u + 1)
                zero(a)
                load_bias(acc[0:1, a, :], col, a)

            start_sum(0)
            for u, (col, a) in enumerate(POOL_UNITS):
                if col == GT2:
                    start_sum(u)
                pool.wait_ge(bias_loaded[a], 32 + 16 * (u // 2 + 1))
                for k in range(KT):
                    n = u * KT + k
                    pool.wait_ge(ada_scaled, n + 1)
                    nc.gpsimd.tensor_tensor(acc[:, a, :], ada_slots[ada_slot(n)], acc[:, a, :], ALU.add).then_inc(ada_used, 1)
                    pool.wait_ge(ada_used, n + 1)
                    if n in (KT // 2, KT + KT // 2):
                        start_sum(u + 1)
                    if n == 3 * KT + 3:
                        pool.wait_ge(squares, 2 + 2 * STRIPS)
                        nc.gpsimd.memset(f_acc[:, :, :], 0.0).then_inc(f_zeroed, 1)
            pool.wait_ge(gfin_loaded, 16)
            for i, (t, n) in enumerate(POOL_PIECES):
                cols = slice(n * TOK_COLS, (n + 1) * TOK_COLS)
                pool.wait_ge(act_scaled, i + 1)
                nc.gpsimd.tensor_tensor(x_sb[:, t, cols], x_sb[:, t, cols], acc[:, 0, cols], ALU.mult).then_inc(pool_out, 1)

        @block.scalar
        def _(act):
            act.dma_start(vec_rows[V_MIX:V_MIX + KT, :], g_mix.rearrange("a (k p) -> (a k) p", p=P)).then_inc(vec_loaded, 16)
            act.dma_start(vec_rows[V_FFN:V_FFN + KT, :], g_ffn.rearrange("a (k p) -> (a k) p", p=P)).then_inc(vec_loaded, 16)
            act.dma_start(vec_rows[V_BETA:V_BETA + 8, :], beta_attn.rearrange("a (k p) -> (a k) p", p=P)).then_inc(vec_loaded, 16)
            act.dma_start(vec_rows[V_GRET:V_GRET + 8, :], g_ret.rearrange("a (k p) -> (a k) p", p=P)).then_inc(vec_loaded, 16)
            act.dma_start(vec_rows[V_C:V_C + KT, :], c.rearrange("a (k p) -> (a k) p", p=P)).then_inc(vec_loaded, 16)
            act.dma_start(cst[:, :], consts).then_inc(cst_loaded, 16)
            act.dma_start(x_sb[:, :, :], x_v).then_inc(x_loaded, 16)
            act.dma_start(sink_row, sinks.to_broadcast([P, 16])).then_inc(sinks_loaded, 16)

            act.wait_ge(x_loaded, 16)
            for t in range(TT):
                nc.scalar.activation(act_hl[:, 4 * t:4 * t + 4, :], x_sb[:, t, :].rearrange("p (k n) -> p k n", k=4), ACT.Square,
                                     accum_out=sq_sum[:, t:t + 1]).then_inc(squares, 1)

            def root(dst, src, n):
                act.wait_ge(var_ready, n)
                nc.scalar.activation(dst, src, ACT.Sqrt).then_inc(std_ready, 1)

            root(std, mean_sq, 1)
            for r in range(8):
                act.wait_ge(turned, r + 1)
                nc.scalar.activation(xn_T[:, 2 * r:2 * r + 2, :], ps[:, r % 4, :].rearrange("p (k n) -> p k n", k=2),
                                     ACT.Copy).then_inc(turned_out, 1)

            def round_group(g, slot, ring, i_fill):
                act.wait_ge(stage_full[slot], 16 * i_fill)
                if not isinstance(g, int) or g >= 2:
                    act.wait_ge(group_used, g - 1)
                nc.scalar.activation(w_hi[:, ring, :], stage[:, slot, :], ACT.Copy).then_inc(hi_ready, 1)

            def static_group(g):
                item = ITEM_OF_GROUP[g] if g < G_MLP else PRE + g
                round_group(g, item % STAGES, g % 2, item // STAGES + 1)

            def modulated_head(half):
                for q in range(2 * half, 2 * half + 2):
                    act.wait_ge(h_ready, 4 * q + 4)
                    nc.scalar.activation(act_hl[:, 4 * q:4 * q + 4, 0:T], xn_T[:, 4 * q:4 * q + 4, :], ACT.Copy).then_inc(mod_hi, 1)

            static_group(0)
            act.wait_ge(squares, 2)
            modulated_head(0)
            static_group(1)

            def copy_gate(n, spread):
                act.wait_ge(gate_spread, spread)
                if spread > 1:
                    act.wait_ge(x_updated, TT * (spread - 1))
                nc.scalar.activation(tmp.rearrange("p a n -> p (a n)"), ps[:, n % 2, :], ACT.Copy).then_inc(gate_copied, 1)

            squared = [TT]

            def row_squares(n, junk):
                for t in range(TT):
                    act.wait_ge(x_updated, squared[0] - TT + 1)
                    act.wait_ge(squares, squared[0])
                    nc.scalar.activation(junk, x_sb[:, t, n * 512:(n + 1) * 512], ACT.Square,
                                         accum_out=sq_sum[:, 4 * t + n:4 * t + n + 1]).then_inc(squares, 1)
                    squared[0] += 1

            def copy_cross(used, pair):
                act.wait_ge(group_used, used)
                nc.scalar.activation(tmp[:, :, :], ps_job[:, 2 * pair:2 * pair + 2, T:2 * T], ACT.Copy).then_inc(cross_copied, 1)

            def scale_tile(slot, k, fill):
                act.wait_ge(ada_full[slot], 16 * fill)
                nc.scalar.activation(ada_slots[slot], ada_slots[slot], ACT.Copy, scale=vec_T[:, bass.ds(V_C + k, 1)]).then_inc(ada_scaled, 1)

            def keep_half(j):
                act.wait_ge(group_used, FIRST[j + 1])
                if JOBS[j][1] == GR0:
                    act.wait_ge(act_ready, 2)
                nc.scalar.activation(result_of(j), psum_of(j), ACT.Copy).then_inc(evacuated, 1)

            def exps(b):
                act.wait_ge(logits_ready, b + 1)
                for t in range(TT):
                    nk, at = key_count(t), 256 * t
                    for e in range(2):
                        s = slice(at + e * nk, at + (e + 1) * nk)
                        i = 2 * t + e
                        nc.scalar.activation(probs[b % 2][:, s], probs[b % 2][:, s], ACT.Exp, bias=nmax[:, i:i + 1], accum_out=p_sum[:, i:i + 1]).then_inc(exp_done, 1)
                nc.scalar.activation(p_sink, d_sink, ACT.Exp).then_inc(exp_done, 1)

            def copy_probs_T(b):
                act.wait_ge(probs_turned, b + 1)
                if b:
                    act.wait_ge(pv_done, b)
                nc.scalar.activation(probs_T[:, 256:768], ps[:, 2, :], ACT.Copy).then_inc(probs_T_ready, 1)
                nc.scalar.activation(probs_T[:, 0:256], ps[:, 3, 0:256], ACT.Copy).then_inc(probs_T_ready, 1)

            def attention_head(b):
                act.wait_ge(pv_done, b + 1)
                if b == 0:
                    act.wait_ge(group_used, G_B)
                nc.scalar.activation(act_hl[:, b, 0:T], ps[:, 3, 256:512], ACT.Copy, scale=vec_T[:, V_BETA + b:V_BETA + b + 1]).then_inc(att_hi, 1)

            def retention_head(h):
                act.wait_ge(ret_turned, h + 1)
                if h == 0:
                    act.wait_ge(group_used, G_OA)
                for e in range(2):
                    k = 2 * h + e
                    nc.scalar.activation(act_hl[:, PAIRS + k, 0:T], ps[:, h, e * T:(e + 1) * T], ACT.Copy,
                                         scale=vec_T[:, V_GRET + k:V_GRET + k + 1]).then_inc(ret_hi, 1)

            for j in range(J_MLP):
                for q in range(N_GROUPS[j]):
                    g = FIRST[j] + q
                    if g >= 2:
                        static_group(g)
                    if g - 2 in LAST_GROUP[:J_B]:
                        keep_half(LAST_GROUP.index(g - 2))
                    if g == G_B:
                        modulated_head(1)
                    if g == G_B + 3:
                        act.wait_ge(kv_spread, 2)
                        nc.scalar.activation(k_dup[:, :, :], ps[:, 0, :].rearrange("p (k n) -> p k n", k=2), ACT.Copy,
                                             scale=float(HEAD) ** -0.5).then_inc(scaled_keys, 1)
                    if pair_at(g, 8) is not None:
                        attention_head(pair_at(g, 8))
                    if pair_at(g, 4) is not None:
                        exps(pair_at(g, 4))
                    if pair_at(g, 7) is not None:
                        copy_probs_T(pair_at(g, 7))
                    if g in (LAST_GROUP[J_BGR] + 3, LAST_GROUP[J_BGR + 1] + 3):
                        n = (g - LAST_GROUP[J_BGR] - 3) // 2
                        act.wait_ge(evacuated, J_BGR + n + 1)
                        cols = slice(n * TOK_COLS, (n + 1) * TOK_COLS)
                        if n == 0:
                            act.wait_ge(scores_done, PAIRS)
                        nc.scalar.activation(gate_sig[:, :, cols], gate[:, :, cols], ACT.Exp, scale=-1.0).then_inc(gate_exp, 1)
                    if g == G_OA + 4:
                        root(gn_std, gn_var, 2)
                    if g in (G_OA + 6, G_OA + 7):
                        retention_head(2 * (g - G_OA - 6))
                        retention_head(2 * (g - G_OA - 6) + 1)
                    if j > J_OR and q == 1:
                        row_squares(j - 1 - J_OR, v_ret[:, 0, 0, :])
                    if j >= J_OR and q == 1:
                        copy_gate(j - J_OR, j - J_OR + 1)
                    for n in range(ada_before(g - 1) if g else 0, ada_before(g)):
                        scale_tile(ada_slot(n), n % KT, ada_fill(n))
            static_group(G_MLP)
            row_squares(STRIPS - 1, v_ret[:, 0, 0, :])
            root(std, mean_sq, 3)
            static_group(G_MLP + 1)
            act.wait_ge(mod_ready, 4)
            for k in range(KT):
                if k % 2 == 0:
                    act.wait_ge(turned, 8 + k // 2 + 1)
                nc.scalar.activation(h2_T[:, k, :], ps[:, (k // 2) % 4, (k % 2) * T:(k % 2 + 1) * T], ACT.Identity,
                                     bias=shift2[:, k:k + 1], scale=scale2[:, k:k + 1]).then_inc(h_ready, 1)

            def fills(g0, u):
                return (PRE + g0 + u) // STAGES + 1

            def hidden_cross(n, used, pair):
                if isinstance(n, int) and n == 0:
                    act.wait_ge(x_updated, TT * STRIPS)
                else:
                    act.wait_ge(hid_ready, n)
                copy_cross(used, pair)

            def hidden_head(n, k0):
                act.wait_ge(hid_f32, n + 1)
                nc.scalar.activation(hid_hl[:, bass.ds(k0, 2), 0:T], tmp[:, :, :], ACT.Copy).then_inc(hid_hi, 1)

            PB = J_MLP % 2

            def w1_first(n0, g0, fill0, after_w2):
                for u in range(4):
                    if u >= 2 or after_w2:
                        round_group(g0 + u, (G_MLP + u) % STAGES, u % 2, fill0(u))
                    if not after_w2 and u < 2:
                        scale_tile(ada_slot(3 * KT + u), u, ada_fill(3 * KT + u))
                    if u == 2:
                        hidden_cross(n0, g0 + 2, PB)
                    if u == 3:
                        hidden_head(n0, 0)

            def w1_two(n0, g0, fill0, m, first=False):
                for u in range(4):
                    jj, q = u // 2, u % 2
                    round_group(g0 + 4 + u + m * 4, (G_MLP + u) % STAGES, q, fill0(u) + 1 + m)
                    if q == 0:
                        hidden_cross(n0 + 1 + jj + m * 2, g0 + 4 + 2 * jj + m * 4, (PB + 1 + jj) % 2)
                    else:
                        hidden_head(n0 + 1 + jj + m * 2, m * 4 + 2 + 2 * jj)
                        if first:
                            scale_tile(ada_slot(3 * KT + 2 + jj), 2 + jj, ada_fill(3 * KT + 2 + jj))

            def w1_rest(n0, g0, fill0, m0=0):
                with act.Fori(m0, F_JOBS // 2 - 1) as m:
                    w1_two(n0, g0, fill0, m)

            w1_first(0, G_MLP, lambda u: fills(G_MLP, u), False)
            w1_two(0, G_MLP, lambda u: fills(G_MLP, u), 0, True)
            w1_rest(0, G_MLP, lambda u: fills(G_MLP, u), 1)

            def w2_block(g0, fill0, n_last, last, s=None):
                for jj in range(STRIPS):
                    for q in range(T_GROUPS):
                        u = 4 * jj + q
                        round_group(g0 + u, (G_MLP + u) % STAGES, u % 2, fill0(q) + jj)
                        if jj == 0 and q == 0:
                            hidden_cross(n_last, g0, (PB + 1) % 2)
                        if jj == 0 and q == 1:
                            hidden_head(n_last, KT - 2)
                        if not last and q == 1:
                            scale_tile(ada_slot(3 * KT + 4 + jj), s * 4 + 4 + jj, s * 2 + ada_fill(3 * KT + 4 + jj))
                        if last and jj > 0 and q == 1:
                            row_squares(jj - 1, act_hl[:, 0, :])
                        if last and q == 2:
                            if jj == 0:
                                act.wait_ge(hid_ready, n_last + 1)
                            copy_gate(jj, STRIPS + jj + 1)

            with act.Fori(0, SUPER - 1) as s:
                g0 = G_MLP + 16 + s * 32
                w2_block(g0, lambda q: (PRE + G_MLP + 16 + q) // STAGES + 1 + s * 8, 7 + s * 8, False, s)
                g1 = G_MLP + 32 + s * 32
                fill1 = lambda u: (PRE + G_MLP + 32 + u) // STAGES + 1 + s * 8
                n1 = 8 + s * 8
                w1_first(n1, g1, fill1, True)
                w1_rest(n1, g1, fill1)
            gl = G_MLP + 16 + 32 * (SUPER - 1)
            w2_block(gl, lambda q: (PRE + gl + q) // STAGES + 1, 8 * SUPER - 1, True)
            row_squares(STRIPS - 1, act_hl[:, 0, :])
            root(std, mean_sq, 4)
            act.wait_ge(normed, 3)
            for t, n in POOL_PIECES:
                cols = slice(n * TOK_COLS, (n + 1) * TOK_COLS)
                nc.scalar.activation(x_sb[:, t, cols], x_sb[:, t, cols], ACT.Copy, scale=rstd[:, t:t + 1]).then_inc(act_scaled, 1)

        @block.tensor
        def _(pe):
            pe.wait_ge(vec_loaded, 80)
            pe.wait_ge(cst_loaded, 16)
            nc.tensor.transpose(ps[:, 0, 0:64], vec_rows[:, :], ident[0:64, 0:64]).then_inc(vec_turned, 1)

            def turn_normed(first):
                for r in range(8):
                    if first and r == 0:
                        pe.wait_ge(vec_ready, 1)
                    if r >= 4 and first:
                        pe.wait_ge(turned_out, r - 3)
                    elif r >= 4:
                        pe.wait_ge(h_ready, KT + 2 * (r - 4) + 2)
                    for e in range(2):
                        for t in range(TT):
                            k = 2 * r + e
                            last = nc.tensor.matmul(ps[:, r % 4, e * T + t * P:e * T + (t + 1) * P], x_sb[:, t, k * P:(k + 1) * P],
                                                    diag[:, t, :], start=True, stop=True)
                    last.then_inc(turned, 1)

            pe.wait_ge(normed, 1)
            turn_normed(True)

            def sum_mod(a, bank, col):
                for k in range(KT):
                    last = nc.tensor.matmul(ps[:, bank, col + k:col + k + 1], acc[:, a, k * P:(k + 1) * P], ones[:, 0:1], start=True, stop=True)
                last.then_inc(mod_summed, 1)

            pe.wait_ge(ones_set, 1)
            pe.wait_ge(turned_out, 8)
            pe.wait_ge(lo_ready, ITEM_OF_TILE[KT - 1] + 1)
            sum_mod(0, 0, 0)

            def half_feature_group(j, k0, ring):
                for e in range(2):
                    o = ps_job[:, banks(j)[0], e * T:(e + 1) * T]
                    for k in range(8):
                        ws = slice(k * FEAT_COLS + e * P, k * FEAT_COLS + (e + 1) * P)
                        nc.tensor.matmul(o, w_hi[:, ring, ws], act_hl[:, k0 + k, 0:T], start=(k == 0), stop=False)
                        nc.tensor.matmul(o, w_hi[:, ring, ws], act_hl[:, k0 + k, T:2 * T], start=False, stop=False)
                        last = nc.tensor.matmul(o, w_lo[:, ring, ws], act_hl[:, k0 + k, 0:T], start=False, stop=(k == 7))
                last.then_inc(group_used, 1)

            def feature_group(k0, ring, pair, last_group):
                for k in range(8):
                    kt = k0 + k
                    for e in range(2):
                        o = ps_job[:, 2 * pair + e, :]
                        ws = slice(k * FEAT_COLS + e * P, k * FEAT_COLS + (e + 1) * P)
                        nc.tensor.matmul(o, w_hi[:, ring, ws], act_hl[:, kt, :], start=(kt == 0), stop=False)
                        last = nc.tensor.matmul(o[:, T:2 * T], w_lo[:, ring, ws], act_hl[:, kt, 0:T], start=False,
                                                stop=last_group and k == 7)
                last.then_inc(group_used, 1)

            def token_group(src, k0, ring, pair, first_group, last_group):
                for k in range(4):
                    for t in range(TT):
                        o = ps_job[:, 2 * pair + t, :]
                        a_hi = src[:, k0 + k, t * P:(t + 1) * P]
                        a_lo = src[:, k0 + k, T + t * P:T + (t + 1) * P]
                        wh = w_hi[:, ring, k * TOK_COLS:(k + 1) * TOK_COLS]
                        wl = w_lo[:, ring, k * TOK_COLS:(k + 1) * TOK_COLS]
                        nc.tensor.matmul(o, a_hi, wh, start=first_group and k == 0, stop=False)
                        nc.tensor.matmul(o, a_hi, wl, start=False, stop=False)
                        last = nc.tensor.matmul(o, a_lo, wh, start=False, stop=last_group and k == 3)
                last.then_inc(group_used, 1)

            def spread_kv():
                pe.wait_ge(evacuated, J_B + 1)
                for e in range(2):
                    for half in range(2):
                        last = nc.tensor.matmul(ps[half * 64:half * 64 + 64, 0, e * T:(e + 1) * T], ident[:, e * 64:e * 64 + 64],
                                                tmp[:, 0, :], start=True, stop=True, skip_group_check=True)
                last.then_inc(kv_spread, 1)
                for t in range(TT):
                    last = nc.tensor.transpose(ps[:, 1, t * P:(t + 1) * P], tmp[:, 1, t * P:(t + 1) * P], ident)
                last.then_inc(kv_spread, 1)

            def scores(b):
                pe.wait_ge(evacuated, J_BQ + b // 2 + 1)
                if b:
                    pe.wait_ge(logits_ready, b)
                if b == SH2_PAIR:
                    pe.wait_ge(ada_used, KT)
                    sum_mod(0, 0, 384)
                if b == 0:
                    pe.wait_ge(scaled_keys, 1)
                    pe.wait_ge(kv_ready, 1)
                for t in range(TT):
                    nk = key_count(t)
                    for e in range(2):
                        last = nc.tensor.matmul(ps[:, e, P * t:P * t + nk], q_T[64 * e:64 * e + 64, b, t * P:(t + 1) * P],
                                                k_dup[64 * e:64 * e + 64, b // 4, 0:nk], start=True, stop=True)
                last.then_inc(scores_done, 1)

            def turn_probs(b):
                pe.wait_ge(probs_ready, b + 1)
                if b:
                    pe.wait_ge(att_ready, b)
                for e in range(2):
                    for m in range(2):
                        s = slice(256 + e * 256 + m * P, 256 + e * 256 + (m + 1) * P)
                        nc.tensor.transpose(ps[:, 2, e * 256 + m * P:e * 256 + (m + 1) * P], probs[b % 2][:, s], ident)
                for e in range(2):
                    last = nc.tensor.transpose(ps[:, 3, e * P:(e + 1) * P], probs[b % 2][:, e * P:(e + 1) * P], ident)
                last.then_inc(probs_turned, 1)

            def probs_values(b):
                pe.wait_ge(probs_T_ready, 2 * b + 2)
                kv = slice(64 * (b // 4), 64 * (b // 4) + 64)
                for e in range(2):
                    o = ps[64 * e:64 * e + 64, 3, 256:512]
                    nc.tensor.matmul(o[:, 0:P], v_att[:, 0, kv], probs_T[:, e * P:(e + 1) * P], start=True, stop=True)
                    for m in range(2):
                        s = slice(256 + e * 256 + m * P, 256 + e * 256 + (m + 1) * P)
                        last = nc.tensor.matmul(o[:, P:2 * P], v_att[:, m, kv], probs_T[:, s], start=(m == 0), stop=(m == 1))
                last.then_inc(pv_done, 1)

            def ret_qk(h):
                for m in range(2):
                    for e in range(2):
                        o = ps[:, h, 0:T] if m == 0 else ps[:, h, T:T + P]
                        last = nc.tensor.matmul(o, qk_ret[:, PAIRS + 2 * h + e, m * P:(m + 1) * P],
                                                qk_ret[:, 2 * h + e, m * P:T], start=(e == 0), stop=(e == 1))
                last.then_inc(qk_done, 1)

            def ret_values(h):
                v0, v1 = (v_ret[:, h // 2, t, (h % 2) * RET_HEAD:(h % 2 + 1) * RET_HEAD] for t in range(TT))
                nc.tensor.matmul(ps[:, h, 0:256], decay[:, h, 0:P], v0, start=True, stop=True)
                nc.tensor.matmul(ps[:, h, 256:512], decay[:, h, P:2 * P], v0, start=True, stop=False)
                nc.tensor.matmul(ps[:, h, 256:512], decay[:, h, 2 * P:3 * P], v1, start=False, stop=True).then_inc(ret_done, 1)

            def turn_ret(h):
                pe.wait_ge(ret_normed, h + 1)
                for e in range(2):
                    for t in range(TT):
                        last = nc.tensor.transpose(ps[:, h, e * T + t * P:e * T + (t + 1) * P],
                                                   gate[:, t, (2 * h + e) * P:(2 * h + e + 1) * P], ident)
                last.then_inc(ret_turned, 1)

            def spread_gate(n, bank):
                nc.tensor.matmul(ps[:, bank, :], ones[:, :], acc[:, 1, n * 512:(n + 1) * 512], start=True, stop=True).then_inc(gate_spread, 1)

            for j in range(J_MLP):
                kind, _, k0, _ = JOBS[j]
                for q in range(N_GROUPS[j]):
                    g = FIRST[j] + q
                    pe.wait_ge(lo_ready, ITEM_OF_GROUP[g] + 1)
                    if q == 0 and jobs_out_before(j):
                        pe.wait_ge(evacuated, jobs_out_before(j))
                    if g == 0:
                        pe.wait_ge(act_ready, 2)
                    if g == G_B:
                        pe.wait_ge(act_ready, 4)
                    if g == G_OA:
                        pe.wait_ge(att_ready, PAIRS // 2)
                    if g == G_OA + 1:
                        pe.wait_ge(att_ready, PAIRS)
                    if j == J_OR:
                        pe.wait_ge(ret_ready, 4 * q + 4)
                    if kind == "feat":
                        half_feature_group(j, k0, g % 2)
                    else:
                        token_group(act_hl, k0 + 4 * q, g % 2, j % 2, q == 0, q == N_GROUPS[j] - 1)
                    if g == G_B - 2:
                        pe.wait_ge(lo_ready, ITEM_OF_TILE[2 * KT - 1] + 1)
                        sum_mod(1, 2, 0)
                    if g == G_B + 1:
                        spread_kv()
                    if pair_at(g, 6) is not None:
                        probs_values(pair_at(g, 6))
                    if pair_at(g, 5) is not None:
                        turn_probs(pair_at(g, 5))
                    if pair_at(g, 1) is not None:
                        scores(pair_at(g, 1))
                    if g == G_OA:
                        pe.wait_ge(att_ready, PAIRS)
                        for h in range(RET_HEADS):
                            ret_qk(h)
                    if g == G_OA + 1:
                        pe.wait_ge(qk_decayed, RET_HEADS)
                        pe.wait_ge(evacuated, J_OA)
                        for h in range(RET_HEADS):
                            ret_values(h)
                    if g in (G_OA + 4, G_OA + 5):
                        turn_ret(2 * (g - G_OA - 4))
                        turn_ret(2 * (g - G_OA - 4) + 1)
                    if j >= J_OR - 1 and j < J_MLP - 1 and q == 1:
                        n = j + 1 - J_OR
                        if n == 0:
                            pe.wait_ge(ret_ready, 2 * RET_HEADS)
                            pe.wait_ge(ada_used, 2 * KT)
                        if n >= 2:
                            pe.wait_ge(gate_copied, n - 1)
                        spread_gate(n, n % 2)
            pe.wait_ge(ada_used, 3 * KT)
            sum_mod(0, 3, 0)

            pe.wait_ge(mod_ready, 4)
            pe.wait_ge(normed, 2)
            turn_normed(False)

            PB = J_MLP % 2

            def w1_two(g, j, first):
                for jj in range(2):
                    for q in range(2):
                        u = 2 * jj + q
                        pe.wait_ge(lo_ready, PRE + 1 + u + g)
                        if q == 0:
                            pe.wait_ge(evacuated, j - 1 + jj)
                        if first and jj == 0:
                            pe.wait_ge(act_ready, 4 + 2 * (q + 1))
                        feature_group(8 * q, u % 2, (PB + jj) % 2, q == 1)

            def w1_block(g0, j0, first):
                if first:
                    w1_two(g0, j0, True)
                    with pe.Fori(1, F_JOBS // 2) as m:
                        w1_two(g0 + m * 4, j0 + m * 2, False)
                else:
                    with pe.Fori(0, F_JOBS // 2) as m:
                        w1_two(g0 + m * 4, j0 + m * 2, False)

            def w2_block(g0, j0, blocks_done, last):
                for jj in range(STRIPS):
                    for q in range(T_GROUPS):
                        pe.wait_ge(lo_ready, PRE + 1 + 4 * jj + q + g0)
                        if q == 0:
                            pe.wait_ge(evacuated, j0 + jj - 1)
                        if jj == 0 and q == 0:
                            pe.wait_ge(hid_ready, blocks_done - 1)
                        if jj == 0 and q == T_GROUPS - 1:
                            pe.wait_ge(hid_ready, blocks_done)
                        token_group(hid_hl, 4 * q, q % 2, (PB + jj) % 2, q == 0, q == T_GROUPS - 1)
                        if last and q == 0:
                            if jj == 0:
                                pe.wait_ge(ada_used, 4 * KT)
                            if jj >= 2:
                                pe.wait_ge(gate_copied, STRIPS + jj - 1)
                            spread_gate(jj, jj % 2)

            w1_block(G_MLP, J_MLP, True)
            with pe.Fori(0, SUPER - 1) as s:
                w2_block(G_MLP + 16 + s * 32, J_MLP + 8 + s * 12, 8 + s * 8, False)
                w1_block(G_MLP + 32 + s * 32, J_MLP + 12 + s * 12, False)
            w2_block(G_MLP + 16 + 32 * (SUPER - 1), J_MLP + 8 + 12 * (SUPER - 1), 8 * SUPER, True)

        @block.vector
        def _(dve):
            steps = [0]

            def link(ins):
                steps[0] += 1
                ins.then_inc(vec_step, 1)
                dve.wait_ge(vec_step, steps[0])

            dve.wait_ge(vec_turned, 1)
            nc.vector.tensor_copy(vec_T, ps[:, 0, 0:64]).then_inc(vec_ready, 1)
            dve.wait_ge(vec_ready, 1)

            def sum_tile(n):
                a, k, item = n // KT, n % KT, ITEM_OF_TILE[n]
                dve.wait_ge(stage_full[item % STAGES], 16 * (item // STAGES + 1))
                if k:
                    dve.wait_ge(lo_ready, ITEM_OF_TILE[n - 1] + 1)
                else:
                    dve.wait_ge(bias_loaded[a], 32)
                nc.vector.scalar_tensor_tensor(out=acc[:, a, :], in0=stage[:, item % STAGES, :], scalar=vec_T[:, V_C + k:V_C + k + 1],
                                               in1=acc[:, a, :], op0=ALU.mult, op1=ALU.add).then_inc(lo_ready, 1)

            def row_norm(total, roots):
                nc.vector.tensor_scalar(mean_sq, total, 1.0 / D, EPS, ALU.mult, ALU.add).then_inc(var_ready, 1)
                dve.wait_ge(std_ready, roots)
                link(nc.vector.reciprocal(rstd, std))
                return refine(rstd, mean_sq, newton[:, 0:2])

            def refine(r, v, step):
                link(nc.vector.tensor_tensor(step, r, r, ALU.mult))
                link(nc.vector.scalar_tensor_tensor(out=step, in0=step, scalar=-0.5, in1=v, op0=ALU.mult, op1=ALU.mult))
                return nc.vector.scalar_tensor_tensor(out=r, in0=step, scalar=1.5, in1=r, op0=ALU.add, op1=ALU.mult)

            def make_diag():
                for t in range(TT):
                    last = nc.vector.tensor_scalar(diag[:, t, :], ident, rstd[:, t:t + 1], None, ALU.mult)
                    if t == 0:
                        link(last)
                last.then_inc(normed, 1)

            for n in range(KT):
                sum_tile(n)
                if n == 6:
                    dve.wait_ge(squares, 2)
                    link(row_norm(sq_sum[:, 0:2], 1))
                    dve.wait_ge(vec_ready, 1)
                    make_diag()
                if n == 9:
                    dve.wait_ge(sinks_loaded, 16)
                    s4 = sink4.rearrange("p (b t e) -> p b t e", b=PAIRS, t=2)
                    n4 = nsink4.rearrange("p (b t e) -> p b t e", b=PAIRS, t=2)
                    for t in range(TT):
                        nc.vector.tensor_copy(s4[:, :, t, :], sink_row.rearrange("p (b e) -> p b e", e=2))
                        link(nc.vector.tensor_scalar(n4[:, :, t, :], sink_row.rearrange("p (b e) -> p b e", e=2), -1.0, None, ALU.mult))

            def take_modulation(half):
                bank, k = 2 * half, 8 * half
                dve.wait_ge(mod_summed, half + 1)
                link(nc.vector.tensor_copy(shift1[:, k:k + 8], ps[:, bank, 0:8]))
                nc.vector.scalar_tensor_tensor(out=scale1[:, k:k + 8], in0=ps[:, bank, 8:16], scalar=1.0, in1=vec_T[:, V_MIX + k:V_MIX + k + 8],
                                               op0=ALU.add, op1=ALU.mult).then_inc(mod_ready, 1)
                dve.wait_ge(mod_ready, half + 1)

            def split_group(g, slot, ring, n_hi):
                dve.wait_ge(hi_ready, n_hi)
                if not isinstance(g, int) or g >= 2:
                    dve.wait_ge(group_used, g - 1)
                nc.vector.tensor_tensor(w_lo[:, ring, :], stage[:, slot, :], w_hi[:, ring, :].bitcast(F32), ALU.subtract).then_inc(lo_ready, 1)

            split_group(0, ITEM_OF_GROUP[0] % STAGES, 0, 1)
            take_modulation(0)
            dve.wait_ge(turned_out, 8)

            def modulate(q):
                for k in range(4 * q, 4 * q + 4):
                    nc.vector.tensor_scalar(xn_T[:, k, :], xn_T[:, k, :], scale1[:, k:k + 1], shift1[:, k:k + 1],
                                            ALU.mult, ALU.add).then_inc(h_ready, 1)

            def modulated_tail(source, q, hi):
                dve.wait_ge(mod_hi, hi)
                nc.vector.tensor_tensor(act_hl[:, 4 * q:4 * q + 4, T:2 * T], source[:, 4 * q:4 * q + 4, :],
                                        act_hl[:, 4 * q:4 * q + 4, 0:T].bitcast(F32), ALU.subtract).then_inc(act_ready, 1)

            modulate(0)
            modulate(1)
            modulated_tail(xn_T, 0, 1)
            modulated_tail(xn_T, 1, 2)

            def sum_cross(dst, pair, crossed):
                dve.wait_ge(cross_copied, crossed)
                nc.vector.tensor_tensor(dst, ps_job[:, 2 * pair:2 * pair + 2, 0:T], tmp[:, :, :], ALU.add).then_inc(evacuated, 1)

            def logits(b):
                dve.wait_ge(scores_done, b + 1)
                if b == SH2_PAIR:
                    dve.wait_ge(mod_summed, 3)
                    nc.vector.tensor_copy(shift2, ps[:, 0, 384:384 + KT]).then_inc(mod_ready, 1)
                for t in range(TT):
                    nk, at = key_count(t), 256 * t
                    for e in range(2):
                        h = 2 * b + e
                        slope = 2.0 ** (-8.0 * (h + 1) / (2 * PAIRS))
                        last = nc.vector.scalar_tensor_tensor(out=probs[b % 2][:, at + e * nk:at + (e + 1) * nk], in0=dist[:, P * t:P * t + nk],
                                                              scalar=float(np.float32(slope)), in1=ps[:, e, P * t:P * t + nk],
                                                              op0=ALU.mult, op1=ALU.add)
                        if (t, e) != (TT - 1, 1):
                            steps[0] += 1
                            last.then_inc(vec_step, 1)
                link(last)
                for t in range(TT):
                    nk, at = key_count(t), 256 * t
                    last = nc.vector.tensor_reduce(mx[:, 2 * t:2 * t + 2], probs[b % 2][:, at:at + 2 * nk].rearrange("p (e n) -> p e n", e=2), AX_X, ALU.max)
                    if t == 0:
                        steps[0] += 1
                        last.then_inc(vec_step, 1)
                link(last)
                link(nc.vector.scalar_tensor_tensor(out=nmax, in0=mx, scalar=-1.0, in1=nsink4[:, 4 * b:4 * b + 4], op0=ALU.mult, op1=ALU.min))
                nc.vector.tensor_tensor(d_sink, sink4[:, 4 * b:4 * b + 4], nmax, ALU.add).then_inc(logits_ready, 1)

            def normalise(b):
                dve.wait_ge(exp_done, 5 * b + 5)
                link(nc.vector.tensor_tensor(p_den, p_sum, p_sink, ALU.add))
                link(nc.vector.reciprocal(p_inv, p_den))
                for t in range(TT):
                    nk, at = key_count(t), 256 * t
                    for e in range(2):
                        i = 2 * t + e
                        s = slice(at + e * nk, at + (e + 1) * nk)
                        last = nc.vector.tensor_scalar(probs[b % 2][:, s], probs[b % 2][:, s], p_inv[:, i:i + 1], None, ALU.mult)
                        if i < 3:
                            steps[0] += 1
                            last.then_inc(vec_step, 1)
                last.then_inc(probs_ready, 1)

            def attention_tail(b):
                dve.wait_ge(att_hi, b + 1)
                nc.vector.scalar_tensor_tensor(out=act_hl[:, b, T:2 * T], in0=ps[:, 3, 256:512], scalar=vec_T[:, V_BETA + b:V_BETA + b + 1],
                                               in1=act_hl[:, b, 0:T].bitcast(F32), op0=ALU.mult, op1=ALU.subtract).then_inc(att_ready, 1)

            def silu_gate(step):
                n, part = step // 3, step % 3
                s = slice(n * TOK_COLS, (n + 1) * TOK_COLS)
                if part == 0:
                    dve.wait_ge(gate_exp, n + 1)
                    link(nc.vector.tensor_scalar(gate_sig[:, :, s], gate_sig[:, :, s], 1.0, None, ALU.add))
                if part < 2:
                    link(nc.vector.reciprocal(gate_sig[:, part, s], gate_sig[:, part, s]))
                else:
                    link(nc.vector.tensor_tensor(gate[:, :, s], gate[:, :, s], gate_sig[:, :, s], ALU.mult))

            def group_stats():
                for h in range(RET_HEADS):
                    dve.wait_ge(ret_done, h + 1)
                    for t in range(TT):
                        i = 2 * h + t
                        steps[0] += 1
                        nc.vector.bn_stats(bn6[:, 6 * i:6 * i + 6], ps[:, h, t * 256:(t + 1) * 256]).then_inc(vec_step, 1)
                dve.wait_ge(vec_step, steps[0])
                for i in range(2 * RET_HEADS):
                    steps[0] += 1
                    nc.vector.bn_aggr(bn2[:, 2 * i:2 * i + 2], bn6[:, 6 * i:6 * i + 6]).then_inc(vec_step, 1)
                dve.wait_ge(vec_step, steps[0])
                nc.vector.tensor_scalar(gn_var, bn2.rearrange("p (i m) -> p i m", m=2)[:, :, 1], EPS, None, ALU.add).then_inc(var_ready, 1)

            def group_norm(h):
                if h == 0:
                    dve.wait_ge(std_ready, 2)
                    link(nc.vector.reciprocal(gn_rstd, gn_std))
                    link(refine(gn_rstd, gn_var, newton))
                for t in range(TT):
                    i = 2 * h + t
                    s = gate[:, t, h * RET_HEAD:(h + 1) * RET_HEAD]
                    steps[0] += 1
                    nc.vector.scalar_tensor_tensor(out=s, in0=ps[:, h, t * 256:(t + 1) * 256], scalar=bn2[:, 2 * i:2 * i + 1],
                                                   in1=s, op0=ALU.subtract, op1=ALU.mult).then_inc(vec_step, 1)
                dve.wait_ge(vec_step, steps[0])
                for t in range(TT):
                    i = 2 * h + t
                    s = gate[:, t, h * RET_HEAD:(h + 1) * RET_HEAD]
                    last = nc.vector.tensor_scalar(s, s, gn_rstd[:, i:i + 1], None, ALU.mult)
                    if t == 0:
                        steps[0] += 1
                        last.then_inc(vec_step, 1)
                last.then_inc(ret_normed, 1)

            def retention_tail(h):
                dve.wait_ge(ret_hi, 2 * h + 2)
                for e in range(2):
                    k = 2 * h + e
                    nc.vector.scalar_tensor_tensor(out=act_hl[:, PAIRS + k, T:2 * T], in0=ps[:, h, e * T:(e + 1) * T],
                                                   scalar=vec_T[:, V_GRET + k:V_GRET + k + 1], in1=act_hl[:, PAIRS + k, 0:T].bitcast(F32),
                                                   op0=ALU.mult, op1=ALU.subtract).then_inc(ret_ready, 1)

            def gated_strip(part, n, spread):
                s = slice(n * 512, (n + 1) * 512)
                dve.wait_ge(gate_copied, spread)
                gate_n = tmp.rearrange("p a n -> p (a n)")
                dve.wait_ge(x_reloaded, 16)
                steps[0] += 1
                for t in range(TT):
                    last = nc.vector.tensor_tensor(part[:, t, s], part[:, t, s], gate_n, ALU.mult)
                    if t == 0:
                        last.then_inc(vec_step, 1)
                link(last)
                link(nc.vector.tensor_tensor(x_sb[:, :, s], x_sb[:, :, s], part[:, :, s], ALU.add))

            def add_residual(part, n, j, pair, used):
                s = slice(n * 512, (n + 1) * 512)
                gate_n = tmp.rearrange("p a n -> p (a n)")
                dve.wait_ge(group_used, used)
                steps[0] += 1
                nc.vector.tensor_tensor(part[:, 0, s], ps_job[:, 2 * pair, :], gate_n, ALU.mult).then_inc(vec_step, 1)
                nc.vector.tensor_tensor(part[:, 1, s], ps_job[:, 2 * pair + 1, :], gate_n, ALU.mult).then_inc(evacuated, 1)
                dve.wait_ge(vec_step, steps[0])
                nc.vector.tensor_tensor(x_sb[:, 0, s], x_sb[:, 0, s], part[:, 0, s], ALU.add).then_inc(x_updated, 1)
                dve.wait_ge(evacuated, j + 1)
                nc.vector.tensor_tensor(x_sb[:, 1, s], x_sb[:, 1, s], part[:, 1, s], ALU.add).then_inc(x_updated, 1)

            def take_out(j):
                kind, c0, k0, nk = JOBS[j]
                pair = j % 2
                if kind == "out_ret":
                    add_residual(y_part, j - J_OR, j, pair, FIRST[j + 1])
                    return
                dve.wait_ge(group_used, FIRST[j + 1])
                if kind == "out_attn":
                    nc.vector.tensor_copy(y_part[:, :, c0:c0 + TOK_COLS], psum_of(j)).then_inc(evacuated, 1)
                elif nk == KT:
                    nc.vector.tensor_copy(result_of(j), psum_of(j)).then_inc(evacuated, 1)
                else:
                    if j == J_B:
                        dve.wait_ge(evacuated, J_B)
                    dst = tmp[:, :, :] if j == J_B else result_of(j)
                    nc.vector.tensor_tensor(dst, psum_of(j), result_of(j), ALU.add).then_inc(evacuated, 1)

            for j in range(J_MLP):
                for q in range(N_GROUPS[j]):
                    g = FIRST[j] + q
                    for i in range(ITEM_OF_GROUP[g - 1] + 1 if g else 0, ITEM_OF_GROUP[g]):
                        if g:
                            sum_tile(ITEMS[i][1])
                    if g:
                        split_group(g, ITEM_OF_GROUP[g] % STAGES, g % 2, g + 1)
                    if pair_at(g, 8) is not None:
                        attention_tail(pair_at(g, 8))
                    if g - 2 in LAST_GROUP[J_B:J_OR]:
                        take_out(LAST_GROUP.index(g - 2))
                    if g - 1 in LAST_GROUP[J_OR:]:
                        take_out(LAST_GROUP.index(g - 1))
                    if g == G_B - 1:
                        take_modulation(1)
                        modulate(2)
                        modulate(3)
                    if g == G_B:
                        modulated_tail(xn_T, 2, 3)
                        modulated_tail(xn_T, 3, 4)
                    if pair_at(g, 4) is not None:
                        normalise(pair_at(g, 4))
                    if g == G_B + 3:
                        dve.wait_ge(kv_spread, 2)
                        nc.vector.tensor_copy(v_att[:, :, :], ps[:, 1, 0:256].rearrange("p (t n) -> p t n", t=2)).then_inc(kv_ready, 1)
                    if pair_at(g, 3) is not None:
                        logits(pair_at(g, 3))
                    if g == G_OA + 2:
                        dve.wait_ge(decay_loaded, 16)
                        for h in range(RET_HEADS):
                            dve.wait_ge(qk_done, h + 1)
                            nc.vector.tensor_tensor(decay[:, h, :], ps[:, h, 0:384], decay[:, h, :], ALU.mult).then_inc(qk_decayed, 1)
                    for step, at in enumerate(SILU_AT):
                        if g == at:
                            silu_gate(step)
                    if g == G_OA + 3:
                        group_stats()
                    if g in (G_OA + 4, G_OA + 5):
                        group_norm(2 * (g - G_OA - 4))
                        group_norm(2 * (g - G_OA - 4) + 1)
                    if g in (G_OA + 6, G_OA + 7):
                        retention_tail(2 * (g - G_OA - 6))
                        retention_tail(2 * (g - G_OA - 6) + 1)
                    if j >= J_OR and q == 1:
                        gated_strip(y_part, j - J_OR, j - J_OR + 1)
            split_group(G_MLP, G_MLP % STAGES, 0, G_MLP + 1)
            take_out(J_MLP - 1)

            dve.wait_ge(mod_summed, 4)
            nc.vector.scalar_tensor_tensor(out=scale2, in0=ps[:, 3, 0:KT], scalar=1.0, in1=vec_T[:, V_FFN:V_FFN + KT],
                                           op0=ALU.add, op1=ALU.mult).then_inc(mod_ready, 1)
            dve.wait_ge(squares, 2 + 2 * STRIPS)
            link(nc.vector.tensor_reduce(bn2[:, 0:2], sq_sum.rearrange("p (t n) -> p t n", t=TT), AX_X, ALU.add))
            link(row_norm(bn2[:, 0:2], 3))
            make_diag()
            split_group(G_MLP + 1, (G_MLP + 1) % STAGES, 1, G_MLP + 2)
            dve.wait_ge(group_used, G_MLP)
            for q in range(4):
                dve.wait_ge(h_ready, KT + 4 * q + 4)
                nc.vector.tensor_copy(act_hl[:, 4 * q:4 * q + 4, 0:T], h2_T[:, 4 * q:4 * q + 4, :]).then_inc(mod_hi, 1)
                modulated_tail(h2_T, q, 4 + q + 1)

            PB = J_MLP % 2

            def hidden(n, crossed, j_done, pair):
                sum_cross(tmp[:, :, :], pair, crossed)
                dve.wait_ge(evacuated, j_done)
                nc.vector.scalar_tensor_tensor(out=tmp[:, :, :], in0=tmp[:, :, :], scalar=0.0, in1=tmp[:, :, :],
                                               op0=ALU.max, op1=ALU.mult).then_inc(hid_f32, 1)

            def hidden_tail(n, k0):
                dve.wait_ge(hid_hi, n + 1)
                nc.vector.tensor_tensor(hid_hl[:, bass.ds(k0, 2), T:2 * T], tmp[:, :, :], hid_hl[:, bass.ds(k0, 2), 0:T].bitcast(F32),
                                        ALU.subtract).then_inc(hid_ready, 1)

            def add_strip(jj, used, pair):
                s = slice(jj * 512, (jj + 1) * 512)
                dve.wait_ge(group_used, used)
                dve.wait_ge(f_zeroed, 1)
                nc.vector.tensor_tensor(f_acc[:, :, s], f_acc[:, :, s], ps_job[:, 2 * pair:2 * pair + 2, :], ALU.add).then_inc(evacuated, 1)

            def w1_rest(n0, g0, j0):
                with dve.Fori(0, F_JOBS // 2 - 1) as m:
                    for jj in range(2):
                        for q in range(2):
                            u = 2 * jj + q
                            g = g0 + 4 + u + m * 4
                            split_group(g, (G_MLP + u) % STAGES, u % 2, g + 1)
                            n = n0 + 1 + jj + m * 2
                            if q == 0:
                                hidden(n, 1 + n, j0 + 2 + jj + m * 2, (PB + 1 + jj) % 2)
                            else:
                                hidden_tail(n, m * 4 + 2 + 2 * jj)

            def w1_first(n0, g0, j0, after_w2):
                for u in range(4):
                    if u >= 2 or after_w2:
                        split_group(g0 + u, (G_MLP + u) % STAGES, u % 2, g0 + u + 1)
                    if u == 0 and after_w2:
                        add_strip(STRIPS - 1, g0, (PB + 1) % 2)
                    if u == 2:
                        hidden(n0, 1 + n0, j0 + 1, PB)
                    if u == 3:
                        hidden_tail(n0, 0)

            def w2_block(g0, j0, n_last, last):
                for jj in range(STRIPS):
                    for q in range(T_GROUPS):
                        u = 4 * jj + q
                        split_group(g0 + u, (G_MLP + u) % STAGES, u % 2, g0 + u + 1)
                        if jj == 0 and q == 0:
                            hidden(n_last, 1 + n_last, j0, (PB + 1) % 2)
                        if jj == 0 and q == 1:
                            hidden_tail(n_last, KT - 2)
                        if jj > 0 and q == 0:
                            if last:
                                add_residual(f_acc, jj - 1, j0 + jj - 1, (PB + jj - 1) % 2, g0 + 4 * jj)
                            else:
                                add_strip(jj - 1, g0 + 4 * jj, (PB + jj - 1) % 2)
                        if last and q == 3:
                            gated_strip(f_acc, jj, STRIPS + jj + 1)

            w1_first(0, G_MLP, J_MLP, False)
            w1_rest(0, G_MLP, J_MLP)
            with dve.Fori(0, SUPER - 1) as s:
                w2_block(G_MLP + 16 + s * 32, J_MLP + 8 + s * 12, 7 + s * 8, False)
                w1_first(8 + s * 8, G_MLP + 32 + s * 32, J_MLP + 12 + s * 12, True)
                w1_rest(8 + s * 8, G_MLP + 32 + s * 32, J_MLP + 12 + s * 12)
            gl, jl = G_MLP + 16 + 32 * (SUPER - 1), J_MLP + 8 + 12 * (SUPER - 1)
            w2_block(gl, jl, 8 * SUPER - 1, True)
            add_residual(f_acc, STRIPS - 1, jl + 3, (PB + 3) % 2, gl + 16)

            dve.wait_ge(squares, 2 + 4 * STRIPS)
            link(nc.vector.tensor_reduce(bn2[:, 0:2], sq_sum.rearrange("p (t n) -> p t n", t=TT), AX_X, ALU.add))
            row_norm(bn2[:, 0:2], 4).then_inc(normed, 1)
            dve.wait_ge(normed, 3)
            dve.wait_ge(gfin_loaded, 16)
            for t, n in VEC_PIECES:
                cols = slice(n * TOK_COLS, (n + 1) * TOK_COLS)
                nc.vector.scalar_tensor_tensor(out=x_sb[:, t, cols], in0=x_sb[:, t, cols], scalar=rstd[:, t:t + 1],
                                               in1=acc[:, 0, cols], op0=ALU.mult, op1=ALU.mult).then_inc(out_ready, 1)


_INS = ["x", "c", "w_ada", "b_ada", "g_mix", "w_in", "beta_attn", "sinks", "g_ret", "w_out", "g_ffn", "w1", "w2", "g_final"]


def shape_constants():
    tok = np.arange(T)
    consts = np.zeros((P, P + 384), np.float32)
    consts[:, 0:P] = np.eye(P)
    for t in range(TT):
        q = tok[t * P:(t + 1) * P, None]
        k = tok[None, 0:P * (t + 1)]
        behind = q // CHUNK - k // CHUNK
        keep = (behind >= 0) & (behind <= 1)
        consts[:, P + P * t:P + P * t + P * (t + 1)] = np.where(keep, -np.abs(q - k), -1e34)
    log_g = np.log(1.0 - 2.0 ** (-5.0 - np.arange(RET_HEADS, dtype=np.float64)))
    decay = np.zeros((RET_HEADS, P, 384), np.float32)
    k, q = tok[:, None], tok[None, :]
    for h in range(RET_HEADS):
        full = np.where(k // CHUNK <= q // CHUNK, np.exp(log_g[h] * np.abs(q - k)), 0.0) * RET_HEAD ** -0.5
        decay[h, :, 0:T] = full[0:P]
        decay[h, :, T:384] = full[P:T, P:T]
    return consts, decay


def kernel(**inputs):
    import concourse.bacc as _bacc
    from concourse.bass_utils import run_bass_kernel_spmd as _run

    nc = _bacc.Bacc("TRN2", target_bir_lowering=False, num_devices=1)
    arrays = {f"in_{n}": np.ascontiguousarray(inputs[n]) for n in _INS}
    arrays["in_consts"], arrays["in_decay"] = shape_constants()
    args = [nc.dram_tensor(n, a.shape, mybir.dt.from_np(a.dtype), kind="ExternalInput").ap() for n, a in arrays.items()]
    out = nc.dram_tensor("out_y", (1, T, D), F32, kind="ExternalOutput").ap()
    build(nc, *args, out)
    r = _run(nc, [arrays], core_ids=[0])
    return r.results[0]["out_y"]
```
